# Optimizing a Trainium2 kernel written in Bass

```python
import math
import jax
import jax.numpy as jnp
from jax import lax
import numpy as np

'''Hybrid diffusion / flow-matching backbone block over latent tokens with a context prefix.

Inputs:  x (BATCH, SEQ, D_MODEL) latent tokens on a flattened grid (row = t // GRID_W, col = t % GRID_W),
         c (BATCH, D_MODEL) conditioning vector, ctx (BATCH, CTX_LEN, D_MODEL) context tokens,
         c_ctx (D_MODEL,) learned constant conditioning vector for context tokens, plus all weights.
Output:  (BATCH, SEQ, D_MODEL) latent stream after DEPTH layers.
Layer l: half SwiGLU FFN -> token mixing -> half SwiGLU FFN, each sub-layer adaLN-modulated
(shift/scale/gate) and followed by DeepNorm post-LayerNorm: x <- LN(alpha*x + gate*f(modulate(x))).
Even layers: one combined projection feeding Hyena (order 2, bidirectional long conv) and a
bidirectional RG-LRU as parallel head groups, concatenated into one output projection.
Odd layers: multi-head latent attention with decoupled 2-D axial rotary key.
'''

D_MODEL = 1024
BATCH = 1
SEQ = 512
DEPTH = 2

CTX_LEN = 256
GRID_W = 64
N_EVEN = (DEPTH + 1) // 2
N_ODD = DEPTH // 2
N_ADA = 9
D_FF = 2816

HY_WIDTH = 512
RG_WIDTH = 512
EV_IN = 3 * HY_WIDTH + 2 * RG_WIDTH
EV_MIX = HY_WIDTH + RG_WIDTH
HY_SHORT = 3
HY_EMB = 33
HY_BANDS = (HY_EMB - 1) // 2
HY_FILT_HIDDEN = 64
HY_TARGET = 1e-2
HY_DECAY_PCT_SHORT = 0.3
HY_DECAY_PCT_LONG = 1.5
HY_MAX_DECAY = math.log(HY_TARGET) / HY_DECAY_PCT_SHORT
HY_MIN_DECAY = math.log(HY_TARGET) / HY_DECAY_PCT_LONG
HY_SHIFT = 0.05
RG_CONV = 4
RG_PAD_L = 2
RG_PAD_R = 1
RG_BLOCKS = 8
RG_BLOCK_DIM = RG_WIDTH // RG_BLOCKS
RG_C = 8.0

MLA_HEADS = 16
MLA_Q_LORA = 768
MLA_KV_LORA = 256
MLA_NOPE = 64
MLA_ROPE = 32
MLA_V = 64
MLA_IN = MLA_Q_LORA + MLA_KV_LORA + MLA_ROPE
MLA_SCALE = (MLA_NOPE + MLA_ROPE) ** -0.5
ROPE_AXIS_PAIRS = MLA_ROPE // 4
ROPE_BASE = 10000.0
Q_BLOCK = 128

ALPHA = (2.0 * DEPTH) ** 0.25
BETA = (8.0 * DEPTH) ** -0.25
LN_EPS = 1e-6
RMS_EPS = 1e-6
F32 = jnp.float32

kernel_name = 'hybrid_hyena_rglru_mla_prefix_dit'

def layernorm(x, g, b):
    xf = x.astype(F32)
    mu = jnp.mean(xf, axis=-1, keepdims=True)
    var = jnp.mean(jnp.square(xf - mu), axis=-1, keepdims=True)
    return ((xf - mu) * lax.rsqrt(var + LN_EPS) * g + b).astype(x.dtype)

def rmsnorm(x, g):
    xf = x.astype(F32)
    y = xf * lax.rsqrt(jnp.mean(jnp.square(xf), axis=-1, keepdims=True) + RMS_EPS)
    return (y * g).astype(x.dtype)

def modulate(x, shift, scale):
    return x * (1 + scale) + shift

def adaln(cond, w, b):
    m = jax.nn.silu(cond) @ w + b
    return m.reshape(cond.shape[0], N_ADA, D_MODEL).transpose(1, 0, 2)[:, :, None, :]

def half_ffn(x, shift, scale, gate, w_in, w_out, g, b):
    h = modulate(x, shift, scale)
    a, u = jnp.split(h @ w_in, 2, axis=-1)
    y = (jax.nn.silu(a) * u) @ w_out
    return layernorm(ALPHA * x + 0.5 * gate * y, g, b)

def dwconv(x, w, b, pad_l, pad_r):
    L = x.shape[1]
    xp = jnp.pad(x, ((0, 0), (pad_l, pad_r), (0, 0)))
    y = xp[:, 0:L] * w[0]
    for k in range(1, w.shape[0]):
        y = y + xp[:, k:k + L] * w[k]
    return y + b

def hyena_filters(L, w1, b1, w2, b2, w3, sin_freq):
    pos = jnp.arange(L, dtype=F32)
    t = pos / L
    bands = jnp.linspace(1e-4, HY_BANDS - 1, HY_BANDS, dtype=F32)
    ang = (2.0 * math.pi * pos / L)[:, None] * bands[None, :]
    feats = jnp.concatenate([t[:, None], jnp.cos(ang), -jnp.sin(ang)], axis=-1)
    h = jnp.sin(sin_freq[0] * (feats @ w1 + b1))
    h = jnp.sin(sin_freq[1] * (h @ w2 + b2))
    h = (h @ w3).astype(F32).reshape(L, 2, HY_WIDTH)
    deltas = jnp.abs(jnp.linspace(HY_MIN_DECAY, HY_MAX_DECAY, HY_WIDTH, dtype=F32))
    window = jnp.exp(-t[:, None] * deltas[None, :]) + HY_SHIFT
    h = h * window[:, None, :]
    return h[:, 0], h[:, 1]

def bidir_fftconv(u, h_fwd, h_bwd, bias):
    L, C = h_fwd.shape
    k = jnp.concatenate([h_fwd, jnp.zeros((1, C), F32), h_bwd[1:][::-1]], axis=0)
    U = jnp.fft.rfft(u.astype(F32), n=2 * L, axis=1)
    K = jnp.fft.rfft(k, n=2 * L, axis=0)
    y = jnp.fft.irfft(U * K[None], n=2 * L, axis=1)[:, :L]
    return (y + u.astype(F32) * bias).astype(u.dtype)

def hyena(u, conv_w, conv_b, f_w1, f_b1, f_w2, f_b2, f_w3, sin_freq, bias):
    u = dwconv(u, conv_w, conv_b, 1, 1)
    x0, x1, v = jnp.split(u, 3, axis=-1)
    h_fwd, h_bwd = hyena_filters(u.shape[1], f_w1, f_b1, f_w2, f_b2, f_w3, sin_freq)
    return x0 * bidir_fftconv(v * x1, h_fwd, h_bwd, bias)

def rglru_coeffs(xc, a_w, a_b, x_w, x_b, lam):
    B, L, _ = xc.shape
    xb = xc.reshape(B, L, RG_BLOCKS, RG_BLOCK_DIM)
    r = jax.nn.sigmoid(jnp.einsum('blnd,nde->blne', xb, a_w).reshape(B, L, RG_WIDTH) + a_b)
    i = jax.nn.sigmoid(jnp.einsum('blnd,nde->blne', xb, x_w).reshape(B, L, RG_WIDTH) + x_b)
    log_a = -RG_C * r.astype(F32) * jax.nn.softplus(-lam.astype(F32))
    a = jnp.exp(log_a)
    b = jnp.sqrt(-jnp.expm1(2.0 * log_a)) * (i * xc).astype(F32)
    return a, b

def linear_scan(a, b, h0, reverse):
    if h0 is not None:
        first = -1 if reverse else 0
        b = b.at[:, first].add(a[:, first] * h0)

    def combine(e1, e2):
        a1, b1 = e1
        a2, b2 = e2
        return a1 * a2, a2 * b1 + b2

    _, h = lax.associative_scan(combine, (a, b), reverse=reverse, axis=1)
    return h

def even_mixer(h_lat, h_ctx, w_in, w_out, conv_w, conv_b, f_w1, f_b1, f_w2, f_b2, f_w3,
               sin_freq, hy_b, rc_w, rc_b, a_w, a_b, x_w, x_b, lam, need_ctx):
    def split(u):
        return (u[..., :3 * HY_WIDTH], u[..., 3 * HY_WIDTH:3 * HY_WIDTH + RG_WIDTH],
                u[..., 3 * HY_WIDTH + RG_WIDTH:])

    hy_l, rx_l, gate_l = split(h_lat @ w_in)
    hy_c, rx_c, gate_c = split(h_ctx @ w_in)
    xc_l = dwconv(rx_l, rc_w, rc_b, RG_PAD_L, RG_PAD_R)
    xc_c = dwconv(rx_c, rc_w, rc_b, RG_PAD_L, RG_PAD_R)
    rnn_l, rnn_c = [], []
    for d, reverse in enumerate((False, True)):
        a_c, b_c = rglru_coeffs(xc_c, a_w[d], a_b[d], x_w[d], x_b[d], lam[d])
        hc = linear_scan(a_c, b_c, None, reverse)
        h_final = hc[:, 0] if reverse else hc[:, -1]
        a_l, b_l = rglru_coeffs(xc_l, a_w[d], a_b[d], x_w[d], x_b[d], lam[d])
        rnn_l.append(linear_scan(a_l, b_l, h_final, reverse))
        rnn_c.append(hc)

    def merge(hy_u, rnn, gate):
        y_hy = hyena(hy_u, conv_w, conv_b, f_w1, f_b1, f_w2, f_b2, f_w3, sin_freq, hy_b)
        y_rg = (rnn[0] + rnn[1]).astype(gate.dtype) * jax.nn.gelu(gate)
        return jnp.concatenate([y_hy, y_rg], axis=-1) @ w_out

    out_lat = merge(hy_l, rnn_l, gate_l)
    out_ctx = merge(hy_c, rnn_c, gate_c) if need_ctx else None
    return out_lat, out_ctx

def mla_queries(q_c, q_norm, w_q_up):
    B, L, _ = q_c.shape
    q = (rmsnorm(q_c, q_norm) @ w_q_up).reshape(B, L, MLA_HEADS, MLA_NOPE + MLA_ROPE)
    return q[..., :MLA_NOPE], q[..., MLA_NOPE:]

def mla_kv(kv_c, kv_norm, w_kv_up):
    B, L, _ = kv_c.shape
    kv = (rmsnorm(kv_c, kv_norm) @ w_kv_up).reshape(B, L, MLA_HEADS, MLA_NOPE + MLA_V)
    return kv[..., :MLA_NOPE], kv[..., MLA_NOPE:]

def apply_rope(x, cos, sin):
    xs = x.reshape(x.shape[:-1] + (2, 2, ROPE_AXIS_PAIRS))
    x1, x2 = xs[..., 0, :], xs[..., 1, :]
    out = jnp.stack([x1 * cos - x2 * sin, x2 * cos + x1 * sin], axis=-2)
    return out.reshape(x.shape).astype(x.dtype)

def blocked_attention(q_nope, q_rope, k_nope, k_rope, v):
    B, Lq, H, _ = q_nope.shape
    nblk = Lq // Q_BLOCK

    def to_blocks(t):
        return t.reshape(B, nblk, Q_BLOCK, H, t.shape[-1]).swapaxes(0, 1)

    def one_block(qb):
        qn, qr = qb
        s = jnp.einsum('bqhd,bkhd->bhqk', qn, k_nope) + jnp.einsum('bqhr,bkr->bhqk', qr, k_rope)
        p = jax.nn.softmax(s.astype(F32) * MLA_SCALE, axis=-1)
        return jnp.einsum('bhqk,bkhd->bqhd', p.astype(v.dtype), v)

    o = lax.map(one_block, (to_blocks(q_nope), to_blocks(q_rope)))
    return o.swapaxes(0, 1).reshape(B, Lq, H, v.shape[-1])

def odd_mixer(h_lat, h_ctx, w_in, q_norm, kv_norm, w_q_up, w_kv_up, w_out, cos, sin, need_ctx):
    B, L, _ = h_lat.shape
    p_l = h_lat @ w_in
    p_c = h_ctx @ w_in
    q_cl, kv_cl, kr_l = p_l[..., :MLA_Q_LORA], p_l[..., MLA_Q_LORA:MLA_Q_LORA + MLA_KV_LORA], p_l[..., MLA_Q_LORA + MLA_KV_LORA:]
    q_cc, kv_cc, kr_c = p_c[..., :MLA_Q_LORA], p_c[..., MLA_Q_LORA:MLA_Q_LORA + MLA_KV_LORA], p_c[..., MLA_Q_LORA + MLA_KV_LORA:]
    qn_l, qr_l = mla_queries(q_cl, q_norm, w_q_up)
    kn_l, v_l = mla_kv(kv_cl, kv_norm, w_kv_up)
    kn_c, v_c = mla_kv(kv_cc, kv_norm, w_kv_up)
    qr_l = apply_rope(qr_l, cos[:, None], sin[:, None])
    kr_l = apply_rope(kr_l, cos, sin)
    o_l = blocked_attention(qn_l, qr_l,
                            jnp.concatenate([kn_l, kn_c], axis=1),
                            jnp.concatenate([kr_l, kr_c], axis=1),
                            jnp.concatenate([v_l, v_c], axis=1))
    out_lat = o_l.reshape(B, L, MLA_HEADS * MLA_V) @ w_out
    out_ctx = None
    if need_ctx:
        qn_c, qr_c = mla_queries(q_cc, q_norm, w_q_up)
        o_c = blocked_attention(qn_c, qr_c, kn_c, kr_c, v_c)
        out_ctx = o_c.reshape(B, h_ctx.shape[1], MLA_HEADS * MLA_V) @ w_out
    return out_lat, out_ctx

def setup_inputs(seed: int = 0) -> dict:
    key = jax.random.key(seed)
    keys = iter(jax.random.split(key, 48))

    def rnd(shape, std):
        return std * jax.random.normal(next(keys), shape, F32)

    a_base = jax.random.uniform(next(keys), (N_EVEN, 2, RG_WIDTH), F32, 0.9, 0.999) ** (1.0 / RG_C)
    rg_lambda = jnp.log(a_base) - jnp.log1p(-a_base)
    return {
        'x': rnd((BATCH, SEQ, D_MODEL), 1.0),
        'c': rnd((BATCH, D_MODEL), 1.0),
        'ctx': rnd((BATCH, CTX_LEN, D_MODEL), 1.0),
        'c_ctx': rnd((D_MODEL,), 1.0),
        'ada_w': rnd((DEPTH, D_MODEL, N_ADA * D_MODEL), 0.5 * D_MODEL ** -0.5),
        'ada_b': rnd((DEPTH, N_ADA * D_MODEL), 0.01),
        'ln_g': 1.0 + rnd((DEPTH, 3, D_MODEL), 0.02),
        'ln_b': rnd((DEPTH, 3, D_MODEL), 0.02),
        'ffn_w_in': rnd((DEPTH, 2, D_MODEL, 2 * D_FF), D_MODEL ** -0.5),
        'ffn_w_out': rnd((DEPTH, 2, D_FF, D_MODEL), BETA * D_FF ** -0.5),
        'ev_w_in': rnd((N_EVEN, D_MODEL, EV_IN), D_MODEL ** -0.5),
        'ev_w_out': rnd((N_EVEN, EV_MIX, D_MODEL), BETA * EV_MIX ** -0.5),
        'hy_conv_w': rnd((N_EVEN, HY_SHORT, 3 * HY_WIDTH), HY_SHORT ** -0.5),
        'hy_conv_b': rnd((N_EVEN, 3 * HY_WIDTH), 0.02),
        'hy_filt_w1': rnd((N_EVEN, HY_EMB, HY_FILT_HIDDEN), HY_EMB ** -0.5),
        'hy_filt_b1': rnd((N_EVEN, HY_FILT_HIDDEN), 0.1),
        'hy_filt_w2': rnd((N_EVEN, HY_FILT_HIDDEN, HY_FILT_HIDDEN), HY_FILT_HIDDEN ** -0.5),
        'hy_filt_b2': rnd((N_EVEN, HY_FILT_HIDDEN), 0.1),
        'hy_filt_w3': rnd((N_EVEN, HY_FILT_HIDDEN, 2 * HY_WIDTH), 0.1 * HY_FILT_HIDDEN ** -0.5),
        'hy_sin_freq': 1.0 + rnd((N_EVEN, 2, HY_FILT_HIDDEN), 0.02),
        'hy_bias': rnd((N_EVEN, HY_WIDTH), 0.5),
        'rg_conv_w': rnd((N_EVEN, RG_CONV, RG_WIDTH), RG_CONV ** -0.5),
        'rg_conv_b': rnd((N_EVEN, RG_WIDTH), 0.02),
        'rg_a_w': rnd((N_EVEN, 2, RG_BLOCKS, RG_BLOCK_DIM, RG_BLOCK_DIM), RG_BLOCK_DIM ** -0.5),
        'rg_a_b': rnd((N_EVEN, 2, RG_WIDTH), 0.02),
        'rg_x_w': rnd((N_EVEN, 2, RG_BLOCKS, RG_BLOCK_DIM, RG_BLOCK_DIM), RG_BLOCK_DIM ** -0.5),
        'rg_x_b': rnd((N_EVEN, 2, RG_WIDTH), 0.02),
        'rg_lambda': rg_lambda,
        'mla_w_in': rnd((N_ODD, D_MODEL, MLA_IN), D_MODEL ** -0.5),
        'mla_q_norm': 1.0 + rnd((N_ODD, MLA_Q_LORA), 0.02),
        'mla_kv_norm': 1.0 + rnd((N_ODD, MLA_KV_LORA), 0.02),
        'mla_w_q_up': rnd((N_ODD, MLA_Q_LORA, MLA_HEADS * (MLA_NOPE + MLA_ROPE)), MLA_Q_LORA ** -0.5),
        'mla_w_kv_up': rnd((N_ODD, MLA_KV_LORA, MLA_HEADS * (MLA_NOPE + MLA_V)), MLA_KV_LORA ** -0.5),
        'mla_w_out': rnd((N_ODD, MLA_HEADS * MLA_V, D_MODEL), BETA * (MLA_HEADS * MLA_V) ** -0.5),
    }

def reference(x, c, ctx, c_ctx, ada_w, ada_b, ln_g, ln_b, ffn_w_in, ffn_w_out, ev_w_in, ev_w_out,
              hy_conv_w, hy_conv_b, hy_filt_w1, hy_filt_b1, hy_filt_w2, hy_filt_b2, hy_filt_w3,
              hy_sin_freq, hy_bias, rg_conv_w, rg_conv_b, rg_a_w, rg_a_b, rg_x_w, rg_x_b, rg_lambda,
              mla_w_in, mla_q_norm, mla_kv_norm, mla_w_q_up, mla_w_kv_up, mla_w_out):
    L = x.shape[1]
    ROWS = L // GRID_W
    rows = jnp.repeat(jnp.arange(ROWS, dtype=F32), GRID_W)
    cols = jnp.tile(jnp.arange(GRID_W, dtype=F32), ROWS)
    inv_freq = ROPE_BASE ** (-jnp.arange(ROPE_AXIS_PAIRS, dtype=F32) / ROPE_AXIS_PAIRS)
    ang = jnp.stack([rows[:, None] * inv_freq, cols[:, None] * inv_freq], axis=1)
    cos, sin = jnp.cos(ang), jnp.sin(ang)

    x_lat, x_ctx = x, ctx
    for l in range(DEPTH):
        last = l == DEPTH - 1
        m_lat = adaln(c, ada_w[l], ada_b[l])
        m_ctx = adaln(c_ctx[None], ada_w[l], ada_b[l])
        x_lat = half_ffn(x_lat, m_lat[0], m_lat[1], m_lat[2], ffn_w_in[l, 0], ffn_w_out[l, 0], ln_g[l, 0], ln_b[l, 0])
        x_ctx = half_ffn(x_ctx, m_ctx[0], m_ctx[1], m_ctx[2], ffn_w_in[l, 0], ffn_w_out[l, 0], ln_g[l, 0], ln_b[l, 0])
        h_lat = modulate(x_lat, m_lat[3], m_lat[4])
        h_ctx = modulate(x_ctx, m_ctx[3], m_ctx[4])
        if l % 2 == 0:
            e = l // 2
            y_lat, y_ctx = even_mixer(h_lat, h_ctx, ev_w_in[e], ev_w_out[e], hy_conv_w[e], hy_conv_b[e],
                                      hy_filt_w1[e], hy_filt_b1[e], hy_filt_w2[e], hy_filt_b2[e], hy_filt_w3[e],
                                      hy_sin_freq[e], hy_bias[e], rg_conv_w[e], rg_conv_b[e], rg_a_w[e], rg_a_b[e],
                                      rg_x_w[e], rg_x_b[e], rg_lambda[e], not last)
        else:
            o = l // 2
            y_lat, y_ctx = odd_mixer(h_lat, h_ctx, mla_w_in[o], mla_q_norm[o], mla_kv_norm[o], mla_w_q_up[o],
                                     mla_w_kv_up[o], mla_w_out[o], cos, sin, not last)
        x_lat = layernorm(ALPHA * x_lat + m_lat[5] * y_lat, ln_g[l, 1], ln_b[l, 1])
        if not last:
            x_ctx = layernorm(ALPHA * x_ctx + m_ctx[5] * y_ctx, ln_g[l, 1], ln_b[l, 1])
            x_ctx = half_ffn(x_ctx, m_ctx[6], m_ctx[7], m_ctx[8], ffn_w_in[l, 1], ffn_w_out[l, 1], ln_g[l, 2], ln_b[l, 2])
        x_lat = half_ffn(x_lat, m_lat[6], m_lat[7], m_lat[8], ffn_w_in[l, 1], ffn_w_out[l, 1], ln_g[l, 2], ln_b[l, 2])
    return x_lat


_drawn_inputs = setup_inputs


def setup_inputs(seed=0):
    import zlib

    import numpy as np

    out = dict(_drawn_inputs(seed))
    spreads = {}
    factors = {'ctx': 4.536,
     'ada_b': 5.801,
     'hy_conv_b': 8.0,
     'hy_filt_b1': 7.778,
     'hy_filt_b2': 5.338,
     'hy_sin_freq': 8.0,
     'rg_conv_b': 5.022,
     'rg_a_w': 2.687,
     'rg_a_b': 8.0,
     'rg_x_b': 8.0,
     'mla_q_norm': 8.0,
     'mla_kv_norm': 8.0,
     'mla_w_q_up': 6.607}
    for name, (base, spread) in spreads.items():
        noise = np.random.default_rng([zlib.crc32(name.encode()), seed]).standard_normal(out[name].shape)
        drawn = base * np.exp(spread * noise) if base else spread * noise
        out[name] = jnp.asarray(drawn.astype(out[name].dtype))
    for name, factor in factors.items():
        out[name] = (out[name] * factor).astype(out[name].dtype)
    return out
```

```python
import math
from contextlib import ExitStack

import numpy as np

import concourse.bass as bass
from concourse import mybir

P = 128
D = 1024
KC = D // P
LAT, CTX = 512, 256
TOK = LAT + CTX
SEGS = ((0, LAT), (LAT, CTX))
D_FF = 2816
FC = D_FF // P
FI = FC // 2
DEPTH = 2
N_ADA = 9
NM = DEPTH * N_ADA * KC
ALPHA = (2.0 * DEPTH) ** 0.25
LN_EPS = 1e-6

F32 = mybir.dt.float32
F32R = mybir.dt.float32r
ACT = mybir.ActivationFunctionType
ALU = mybir.AluOpType

HY = 512
HC = HY // P
EV_IN = 3 * HY + 2 * HY
RG_BLOCK = 64
HY_EMB = 33
HY_BANDS = (HY_EMB - 1) // 2
FH = 64
TB = TOK // P
LB, CB_ = LAT // P, CTX // P
GAP = 2
GT_ = TOK + GAP
GSEGS = ((0, LAT), (LAT + GAP, CTX))
PADW = GT_ + 6
LAG = 2

MH = 16
NOPE, ROPE, VD = 64, 32, 64
QD = NOPE + ROPE
QL, KVL = 768, 256
QC_, KVC = QL // P, KVL // P
SCALE = QD ** -0.5
GRID_W = 64
QT_ = LAT // P

ADA_RING = 4
ADA_FIRST = 3
COEF_FIRST = 5

VEC = {}


def vec_rows():
    at = 0
    for name, rows in (("ada_b", NM), ("c", KC), ("c_ctx", KC), ("ln_g", DEPTH * 3 * KC), ("ln_b", DEPTH * 3 * KC),
                       ("hy_conv_w", 3 * 3 * HC), ("hy_conv_b", 3 * HC), ("hy_bias", HC), ("rg_conv_w", 4 * HC),
                       ("rg_conv_b", HC), ("rg_a_b", 2 * HC), ("rg_x_b", 2 * HC), ("rg_lambda", 2 * HC),
                       ("mla_q_norm", 6), ("mla_kv_norm", 2)):
        VEC[name] = (at, rows)
        at += rows
    return at


def constants():
    out = {}
    feats, win = [], []
    deltas = np.abs(np.linspace(math.log(1e-2) / 1.5, math.log(1e-2) / 0.3, HY))
    for name, L in (("l", LAT), ("c", CTX)):
        pos = np.arange(L)
        w = 2 * np.pi * (pos[:, None] + 0.5) * pos[None, :] / (2 * L)
        cs = np.stack([np.cos(w), np.sin(w)])
        b = L // P
        out[f"fwd_{name}"] = cs.reshape(2, b, P, b, P).transpose(1, 4, 3, 0, 2)
        out[f"inv_{name}"] = (cs / L).reshape(2, b, P, L).transpose(1, 2, 0, 3)
        t = pos / L
        ang = 2.0 * np.pi * t[:, None] * np.linspace(1e-4, HY_BANDS - 1, HY_BANDS)[None, :]
        feats.append(np.concatenate([t[:, None], np.cos(ang), -np.sin(ang)], -1))
        win.append(np.exp(-t[:, None] * deltas[None, :]) + 0.05)
    out["feats"] = np.concatenate(feats).T
    win = np.concatenate(win).reshape(TB, P, HY)
    winb = win.copy()
    winb[0, 0] = winb[LB, 0] = 0.0
    out["win"] = np.stack([win, winb], 1).transpose(2, 0, 1, 3)
    t = np.arange(LAT)
    inv = 10000.0 ** (-np.arange(ROPE // 4) / (ROPE // 4))
    ang = np.stack([(t // GRID_W)[None, :] * inv[:, None], (t % GRID_W)[None, :] * inv[:, None]])
    cos = np.repeat(np.cos(ang)[:, None], 2, 1).reshape(ROPE, LAT)
    sin = np.stack([-np.sin(ang), np.sin(ang)], 1).reshape(ROPE, LAT)
    out["rope"] = np.concatenate([cos, sin, cos, sin])
    return {k: np.ascontiguousarray(v, dtype=np.float32) for k, v in out.items()}


VROWS = vec_rows()
VT = -(-VROWS // P)


def vec_pieces():
    pieces = []
    for name, (at, rows) in VEC.items():
        done = 0
        while done < rows:
            t, r = (at + done) // P, (at + done) % P
            n = min(rows - done, P - r)
            pieces.append((name, done, t, r, n))
            done += n
    return pieces


def build(nc, A, out):
    stack = ExitStack()

    def sem(name):
        return nc.alloc_semaphore(name)

    BASE = 16512
    free = [BASE]

    def sb(name, shape, dt=F32, at=None):
        size = 4 * int(np.prod(shape[1:]))
        if at is None:
            at = free[0]
            free[0] += -(-size // 32) * 32
        assert at + size <= 229344, (name, at + size - 229344)
        return nc.alloc_sbuf_tensor_at(name, list(shape), dt, offset=at)

    X = sb("X", [P, KC, TOK])
    h_at = free[0]
    HHI = sb("HHI", [P, KC, TOK], F32R)
    HLO = sb("HLO", [P, KC, TOK], F32R)
    SQ = sb("SQ", [P, KC, TOK], F32, at=h_at)
    RAW = [sb(f"RAW{s}", [P, 1024]) for s in range(2)]
    w_at = free[0]
    WHI = {s: sb(f"WHI{s}", [P, 2048], F32R) for s in "AB"}
    WLO = {s: sb(f"WLO{s}", [P, 2048], F32R) for s in "AB"}
    r1 = free[0]
    WHI["W"] = sb("WHIW", [P, 2048], F32R)
    WLO["W"] = sb("WLOW", [P, 2048], F32R)
    GM = {s: sb(f"GM{s}", [P, TOK]) for s in "AB"}
    GHI = {s: sb(f"GHI{s}", [P, TOK], F32R) for s in "AB"}
    GLO = {s: sb(f"GLO{s}", [P, TOK], F32R) for s in "AB"}
    MU = sb("MU", [P, TOK])
    RSTD = sb("RSTD", [P, TOK])
    H32 = sb("H32", [P, 2, LAT])
    r1_end = free[0]
    VECS = sb("VECS", [P, VT * P])
    MOD = sb("MOD", [P, NM, 2])
    NCOEF = DEPTH * 3
    CG = sb("CG", [P, NCOEF + 1, KC, 2])
    CB = sb("CB", [P, NCOEF + 1, KC, 2])
    AG = sb("AG", [P, NCOEF + 1, KC])
    AB = sb("AB", [P, NCOEF + 1, KC])
    GATE = sb("GATE", [P, DEPTH * 3, KC, 2])
    ID = sb("ID", [P, P])
    ONES = sb("ONES", [P, P])
    EPS = sb("EPS", [P, 1])
    ZERO = sb("ZERO", [P, 1])
    SC = sb("SC", [P, KC, 32])
    FVEC = sb("FVEC", [FH, 8])
    SPL = sb("SPL", [P, 8, 2 * HC])
    r2 = free[0]
    ADA = [sb(f"ADA{s}", [P, D]) for s in range(ADA_RING)]
    ADAP = sb("ADAP", [P, D // 4])
    TOP = 229344

    def region(start, end):
        at = [start]

        def place(name, shape, dt=F32):
            size = -(-4 * int(np.prod(shape[1:])) // 32) * 32
            t = sb(name, shape, dt, at=at[0])
            at[0] += size
            assert at[0] <= end, (name, at[0] - end)
            return t
        return place

    place = region(w_at, r1 + 16384)
    XIN = place("XIN", [P, TB, D])
    VIN = place("VIN", [P, VT, P])
    FEATS = place("FEATS", [HY_EMB, TOK])
    FW1 = place("FW1", [HY_EMB, FH])
    FW2 = place("FW2", [FH, FH])
    FW3 = place("FW3", [FH, 2 * HY])
    KOUT = place("KOUT", [P, 2, 2, HY])
    place = region(h_at, h_at + 49152)
    FILT = place("FILT", [P, TB, 2, HY])
    FWDL = place("FWDL", [P, LB, LB, 2, P])
    FWDC = place("FWDC", [P, CB_, CB_, 2, P])
    place = region(r1 + 16384, r1_end)
    WINT = place("WINT", [P, TB, 2, HY])
    place = region(r2 + 17408, TOP)
    FZ = place("FZ", [FH, TOK])
    FN = place("FN", [FH, TOK])
    FS = place("FS", [FH, TOK])
    HF_ = place("HF_", [P, 2, HY])

    place = region(r1, r1_end)
    PAD = [place(f"PAD{n}", [P, PADW]) for n in range(3)]
    XC = place("XC", [P, HC, GT_])
    GATED = place("GATED", [P, HC, GT_])
    T_ = [place(f"RT{n}", [P, GT_]) for n in range(3)]
    place = region(r2, TOP)
    U = place("U", [P, HC, GT_])
    X0 = place("X0", [P, HC, GT_])
    T_ += [place(f"RT{n}", [P, GT_]) for n in range(3, 9)]
    RR, IG, AA, TH = T_[0:2], T_[2:4], T_[4:6], T_[6:8]
    HS = [T_[8], sb("RT9", [P, GT_], F32, at=r1 + 2 * 3104)]
    place = region(w_at, r1)
    UT = place("UT", [P, TB, HY])
    YL = place("YL", [P, 2, LB, HY])
    YC = [place("YC0", [P, CB_, HY]), sb("YC1", [P, CB_, HY], F32, at=r1)]
    SLAB, KFS, TMP, BD = [], [], [], []
    for n in range(2):
        place = region(h_at + 24576 * n, h_at + 24576 * n + 12288)
        SLAB.append(place(f"SLAB{n}", [P, 1024]))
        KFS.append(place(f"KFS{n}", [P, 2, HY]))
        TMP.append(place(f"TMP{n}", [P, HY]))
        BD.append(place(f"BD{n}", [P, 2, P]))
    place = region(r2, TOP)
    ROT = place("ROT", [P, LAT])
    QC = place("QC", [P, QC_, LAT])
    KV = place("KV", [P, KVC, TOK])
    SQQ = place("SQQ", [P, QC_, LAT])
    QRS = place("QRS", [P, LAT])
    KRS = place("KRS", [P, TOK])
    KRT = place("KRT", [P, TOK])
    KR2 = place("KR2", [P, LAT])
    place = region(r1, r1_end)
    QNH, QNL = (place(f"QN{n}", [P, QC_, LAT], F32R) for n in "HL")
    KVH, KVL_ = (place(f"KVN{n}", [P, KVC, TOK], F32R) for n in "HL")
    QH = [place(f"QH{z}", [P, LAT], F32R) for z in range(2)]
    QLO = [place(f"QL{z}", [P, LAT], F32R) for z in range(2)]
    place = region(w_at, r1)
    VRAW = place("VRAW", [P, KVC, MH * VD])
    WVH, WVL = (place(f"WV{n}", [P, KVC, MH * VD], F32R) for n in "HL")
    place = region(h_at, h_at + 49152)
    VH, VL = (place(f"V{n}", [P, TB, MH * VD], F32R) for n in "HL")
    place = region(w_at, r1)
    KH = [place(f"KH{z}", [P, TOK], F32R) for z in range(2)]
    KLO = [place(f"KL{z}", [P, TOK], F32R) for z in range(2)]
    WRAW = [place(f"WRAW{z}", [P, QC_ * QD + KVC * NOPE]) for z in range(2)]
    QT = place("QT", [P, LAT])
    QR2 = place("QR2", [P, LAT])
    VSH = [place(f"VSH{z}", [P, TB, VD], F32R) for z in range(2)]
    VSL = [place(f"VSL{z}", [P, TB, VD], F32R) for z in range(2)]
    OS = [place(f"OS{z}", [VD, CTX]) for z in range(2)]
    WKH = [place(f"WKH{z}", [P, KVC, NOPE], F32R) for z in range(2)]
    WKL = [place(f"WKL{z}", [P, KVC, NOPE], F32R) for z in range(2)]
    place = region(r2 + 2048, TOP)
    PTH = [place(f"PTH{z}", [P, TB, 2 * P], F32R) for z in range(2)]
    PTL = [place(f"PTL{z}", [P, TB, 2 * P], F32R) for z in range(2)]
    PR = [place(f"PR{z}", [P, TOK]) for z in range(2)]
    WQH = [place(f"WQH{z}", [P, QC_, P], F32R) for z in range(2)]
    WQL = [place(f"WQL{z}", [P, QC_, P], F32R) for z in range(2)]
    STAT = [place(f"STAT{z}", [P, 4]) for z in range(2)]
    DIAG = [place(f"DIAG{z}", [P, P]) for z in range(2)]
    place = region(r2 + 2048, TOP)
    OCH = place("OCH", [P, KC, LAT])
    OUT = sb("OUT", [P, LAT // P, D], F32, at=h_at)
    OD = nc.dram_tensor("heads_out", (MH * VD, LAT), F32, kind="Internal").ap()
    KF = nc.dram_tensor("filter_spectra", (LB + CB_, P, 2, HY), F32, kind="Internal").ap()

    PSALL = nc.alloc_psum_tensor("PSALL", [P, 8, 512], F32)
    PS = [PSALL[:, b, :] for b in range(8)]

    vin_in, xin_in = sem("vin_in"), sem("xin_in")
    const_ok = sem("const_ok")
    tr_done, tr_taken = sem("tr_done"), sem("tr_taken")
    cond_ok = sem("cond_ok")
    ada_in = [sem(f"ada_in{s}") for s in range(ADA_RING)]
    ada_used, ada_sum, ada_row, ada_tr, mod_ok = (sem(n) for n in ("ada_used", "ada_sum", "ada_row", "ada_tr", "mod_ok"))
    coef_ok = sem("coef_ok")
    raw_in = [sem(f"raw_in{s}") for s in range(2)]
    hi_done, lo_done = sem("hi_done"), sem("lo_done")
    pe = {s: sem(f"pe_{s}") for s in "ABW"}
    silu = {s: sem(f"silu_{s}") for s in "AB"}
    mul = {s: sem(f"mul_{s}") for s in "AB"}
    ghi = {s: sem(f"ghi_{s}") for s in "AB"}
    glo = {s: sem(f"glo_{s}") for s in "AB"}
    evac = sem("evac")
    ln_pe, ln_mu, ln_cen, ln_sq, ln_std, ln_rstd, ln_n, ln_h32, ln_x = (
        sem(f"ln_{n}") for n in ("pe", "mu", "cen", "sq", "std", "rstd", "n", "h32", "x"))
    flt_in, tab_in, kf_out = sem("flt_in"), sem("tab_in"), [sem(f"kf_out{n}") for n in range(2)]
    f_pe, f_sin, f_dve, f_win, f_filt, f_spec = (sem(f"f_{n}") for n in ("pe", "sin", "dve", "win", "filt", "spec"))
    spl = sem("spl")
    pad_zero, conv, mx_taken = sem("pad_zero"), sem("conv"), sem("mx_taken")
    ut_pe, ut_ok = sem("ut_pe"), sem("ut_ok")
    bd_zero, bd_in = sem("bd_zero"), [sem(f"bd_in{n}") for n in range(2)]
    gate_pe = sem("gate_pe")
    r_sig, r_exp, r_tanh, r_sqrt = (sem(f"r_{n}") for n in ("sig", "exp", "tanh", "sqrt"))
    r_in, r_sq, r_m, r_b, r_scan, r_y, y_rg = (sem(f"r_{n}") for n in ("in", "sq", "m", "b", "scan", "y", "y_rg"))
    slab_in, kfs_in = [sem(f"slab_in{n}") for n in range(2)], [sem(f"kfs_in{n}") for n in range(2)]
    df_pe, df_y, inv_pe, y_hy, hy_t = (sem(n) for n in ("df_pe", "df_y", "inv_pe", "y_hy", "hy_t"))
    m_taken, mr_sq, mr_pe, mr_std, mr_rs, mr_n, mr_hi, mr_lo = (
        sem(f"m_{n}") for n in ("taken", "rms_sq", "rms_pe", "rms_std", "rms_rs", "rms_n", "rms_hi", "rms_lo"))
    rot_in, v_in, v_hi, v_lo, v_pe, v_th, v_tl, kr, krp = (
        sem(n) for n in ("rot_in", "v_in", "v_hi", "v_lo", "v_pe", "v_th", "v_tl", "kr", "krp"))
    wr_in = [sem(f"wr_in{z}") for z in range(2)]
    wq_hi, wq_ok, vs_ok = sem("wq_hi"), sem("wq_ok"), sem("vs_ok")
    q_pe, k_pe, q_rot, q_cp, q_sum, q_hi, q_lo, k_hi, k_lo = (
        sem(n) for n in ("q_pe", "k_pe", "q_rot", "q_cp", "q_sum", "q_hi", "q_lo", "k_hi", "k_lo"))
    s_pe, s_max, s_nb, s_exp, s_inv, s_norm, t_pe, pt_hi, pt_lo, av_pe, o_cp = (
        sem(n) for n in ("s_pe", "s_max", "s_nb", "s_exp", "s_inv", "s_norm", "t_pe", "pt_hi", "pt_lo", "av_pe", "o_cp"))
    o_out = [sem(f"o_out{z}") for z in range(2)]
    och_in, och_hi, och_lo = sem("och_in"), sem("och_hi"), sem("och_lo")
    fin_x, fin_tr, fin_cp = sem("fin_x"), sem("fin_tr"), sem("fin_cp")
    h_hi, h_lo = sem("h_hi"), sem("h_lo")
    out_in = sem("out_in")

    count = dict(q=0, A=0, B=0, W=0, evac=0, g=0, gs=0, ln=0, h=0, tr=0, ada=0, taken=0)

    class Counts:
        def __init__(self, q, A, B, W, evac, g, gs, ln, h, tr, ada, taken):
            self.q, self.A, self.B, self.W, self.evac, self.g = q, A, B, W, evac, g
            self.gs, self.ln, self.h, self.tr, self.ada, self.taken = gs, ln, h, tr, ada, taken

    plan = {}

    def stage(name, **steps):
        plan[name] = Counts(**count)
        for k, v in steps.items():
            count[k] += v

    def ffn_plan(name, S, ada=0):
        stage(name, ada=ada, q=6 * FI, A=S * FI, B=S * FI, W=KC * S * FI, evac=KC * S * FI, g=FI, gs=S * FI)

    def ln_plan(name, S):
        stage(name, ln=S, h=KC * S)

    stage("vec", tr=VT)
    stage("x", tr=2 * KC)
    stage("ada_first", ada=ADA_FIRST)
    stage("h0", h=KC * 2)
    ffn_plan("ffn0", 2, ada=N_ADA - ADA_FIRST)
    ln_plan("ln0", 2)
    stage("ev_in", q=20, A=15, B=15, taken=40)
    stage("ev_out", q=8, A=6, B=6, evac=16)
    ln_plan("ln1", 2)
    ffn_plan("ffn1", 2, ada=N_ADA)
    ln_plan("ln2", 2)
    ffn_plan("ffn2", 2)
    ln_plan("ln3", 2)
    stage("mla_in", q=9, A=3 + 2 + 2, B=2 + 2)
    stage("mla_out", q=8, A=4, B=4, evac=8)
    ln_plan("ln4", 1)
    ffn_plan("ffn3", 1)
    stage("final", ln=1)

    def raw_slot(q):
        return q % 2

    def raw_value(q, i=0, halves=6):
        return 16 * (q // 2 + 1) + i * 8 * halves

    def ffn_halves(last):
        units = [("B", 0), ("A", 1), ("W", 0)]
        if last:
            units = [u for u in units if u != ("A", 1)]
        return [(s, d, h, 2 + 2 * n + h) for n, (s, d) in enumerate(units) for h in range(2)]


    EV_CHUNKS = [c for n in range(4) for c in (12 + n, 16 + n)] + [c for n in range(4) for c in (4 + n, 8 + n)] + [0, 1, 2, 3]
    MLA_COLS = [QL, QL + P, QL + KVL] + [P * n for n in range(QC_)]
    NF = LB + CB_
    FREQ = [(0, b) for b in range(LB)] + [(1, b) for b in range(CB_)]

    MLA_HALF = [0, 2, 3, 5, 7]

    def KR_PARTS(raw, t):
        src = raw[:, 0:KC * ROPE].rearrange("p (k n) -> p k n", k=KC)
        dst = t[:, 0:KC * 2 * ROPE].rearrange("p (k n) -> p k n", k=KC)
        halves = lambda x: x.rearrange("p k (a f j) -> p k a f j", a=2, f=2)
        return [(src, dst[:, :, 0:ROPE])] + [(halves(src)[:, :, :, 1 - f, :], halves(dst[:, :, ROPE:2 * ROPE])[:, :, :, f, :])
                                             for f in range(2)]

    RMS = [(KV, KVC, 0, LAT, KRS, KVL), (KV, KVC, LAT, CTX, KRS, KVL), (QC, QC_, 0, LAT, QRS, QL)]

    def SC_(s):
        return PSALL[:, 2 * (s % 2):2 * (s % 2) + 2, :].rearrange("p b n -> p (b n)")[:, 0:TOK]

    TR_ = PSALL[:, 4:6, :].rearrange("p b n -> p (b n)")[:, 0:TOK].rearrange("p (t n) -> p t n", t=TB)

    SPL_N = 2 + 5 + 14 + 5
    CONVS = [("rg", n) for n in range(HC)] + [("hy", c) for n in range(HC) for c in (4 + n, 8 + n)] + [("hy", n) for n in range(HC)]
    CONV_END = []
    for n, (kind, c) in enumerate(CONVS):
        CONV_END.append((CONV_END[-1] if n else 0) + (4 if kind == "rg" else 4 if 8 <= c else 3))

    def down_groups(S):
        if S == 1:
            return [(m, 0) for m in range(KC)]
        return [(m + d, s) for m in range(0, KC, 2) for s in range(2) for d in range(2)]

    def down_bank(m, s):
        return PS[6 + m % 2][:, 0:LAT] if s == 0 else PS[5][:, CTX * (m % 2):CTX * (m % 2) + CTX]

    block = stack.enter_context(nc.Block())

    @block.sync
    def _(sp):
        rows = {}
        for name, src in (("ada_b", A["ada_b"].rearrange("l (r n) -> (l r) n", n=P)),
                          ("c", A["c"].rearrange("a (r n) -> (a r) n", n=P)),
                          ("c_ctx", A["c_ctx"].rearrange("(r n) -> r n", n=P)),
                          ("ln_g", A["ln_g"].rearrange("l j (r n) -> (l j r) n", n=P)),
                          ("ln_b", A["ln_b"].rearrange("l j (r n) -> (l j r) n", n=P)),
                          ("hy_conv_w", A["hy_conv_w"].rearrange("l j (r n) -> (l j r) n", n=P)),
                          ("hy_conv_b", A["hy_conv_b"].rearrange("l (r n) -> (l r) n", n=P)),
                          ("hy_bias", A["hy_bias"].rearrange("l (r n) -> (l r) n", n=P)),
                          ("rg_conv_w", A["rg_conv_w"].rearrange("l j (r n) -> (l j r) n", n=P)),
                          ("rg_conv_b", A["rg_conv_b"].rearrange("l (r n) -> (l r) n", n=P)),
                          ("rg_a_b", A["rg_a_b"].rearrange("l j (r n) -> (l j r) n", n=P)),
                          ("rg_x_b", A["rg_x_b"].rearrange("l j (r n) -> (l j r) n", n=P)),
                          ("rg_lambda", A["rg_lambda"].rearrange("l j (r n) -> (l j r) n", n=P)),
                          ("mla_q_norm", A["mla_q_norm"].rearrange("l (r n) -> (l r) n", n=P)),
                          ("mla_kv_norm", A["mla_kv_norm"].rearrange("l (r n) -> (l r) n", n=P))):
            rows[name] = src
        for name, first, t, r, n in vec_pieces():
            sp.dma_start(VIN[r:r + n, t, :], rows[name][first:first + n, :]).then_inc(vin_in, 16)
        for n, src in enumerate((A["hy_filt_b1"][0], A["hy_filt_b2"][0], A["hy_sin_freq"][0, 0], A["hy_sin_freq"][0, 1])):
            sp.dma_start(FVEC[:, n:n + 1], src.rearrange("(p a) -> p a", a=1)).then_inc(flt_in, 16)
        for dst, src in ((FEATS, A["feats"]), (FW1, A["hy_filt_w1"][0]), (FW2, A["hy_filt_w2"][0]), (FW3, A["hy_filt_w3"][0])):
            sp.dma_start(dst[:, :], src).then_inc(flt_in, 16)
        for t in range(LAT // P):
            sp.dma_start(XIN[:, t, :], A["x"][0, t * P:(t + 1) * P, :]).then_inc(xin_in, 16)
        for t in range(CTX // P):
            sp.dma_start(XIN[:, LAT // P + t, :], A["ctx"][0, t * P:(t + 1) * P, :]).then_inc(xin_in, 16)

        sp.dma_start(WINT[:, :, :, :], A["win"]).then_inc(tab_in, 16)
        for b in range(LB):
            sp.dma_start(FWDL[:, b, :, :, :], A["fwd_l"][b]).then_inc(tab_in, 16)
        for b in range(CB_):
            sp.dma_start(FWDC[:, b, :, :, :], A["fwd_c"][b]).then_inc(tab_in, 16)

        def ffn_load(w_in, w_out, slot, u, half, q, i=0):
            if not (isinstance(i, int) and q + 6 * i < 2):
                sp.wait_ge(lo_done, q - 1 + 6 * i)
            dst = RAW[raw_slot(q)][:, :]
            if slot == "W":
                src = w_out[bass.ds((2 * u + half) * P, P), :]
            else:
                src = w_in.rearrange("(k p) (c n) -> p k c n", p=P, n=P)[
                    :, :, bass.ds(half * FC + 2 * u + (slot == "B"), 1), :].squeeze(2)
                dst = dst.rearrange("p (k n) -> p k n", k=KC)
            sp.dma_start(dst, src).then_inc(raw_in[raw_slot(q)], 16)

        def ffn(name, w_in, w_out):
            q0 = plan[name].q
            for half in range(2):
                ffn_load(w_in, w_out, "A", 0, half, q0 + half)

            def body(i, last=False):
                for slot, d, half, j in ffn_halves(last):
                    ffn_load(w_in, w_out, slot, i + d, half, q0 + j, i)
            with sp.Fori(0, FI - 1) as i:
                body(i)
            body(FI - 1, last=True)

        ffn("ffn0", A["ffn_w_in"][0, 0], A["ffn_w_out"][0, 0])
        def proj_load(w, chunk, q):
            sp.wait_ge(lo_done, q - 1)
            sp.dma_start(RAW[raw_slot(q)][:, :].rearrange("p (k n) -> p k n", k=KC),
                         w.rearrange("(k p) (c n) -> p k c n", p=P, n=P)[:, :, chunk, :])\
                .then_inc(raw_in[raw_slot(q)], 16)

        for n, c in enumerate(EV_CHUNKS):
            proj_load(A["ev_w_in"][0], c, plan["ev_in"].q + n)
        sp.wait_ge(pe["A"], plan["ev_out"].A)
        sp.wait_ge(pe["B"], plan["ev_out"].B)
        for n in range(2):
            sp.wait_ge(kf_out[n], 16 * NF // 2)
        for n in range(2 * NF - 1):
            if n == 2:
                for m in range(2):
                    proj_load(A["ev_w_out"][0], m, plan["ev_out"].q + m)
            if n >= 2:
                if n < NF + 2:
                    sp.wait_ge(df_y, 4 * (n - 1))
                else:
                    sp.wait_ge(inv_pe, HC + n - NF - 2)
            if n < NF:
                src = (A["fwd_l"][n] if n < LB else A["fwd_c"][n - LB]).rearrange("p t s f -> p (t s f)")
                sp.dma_start(SLAB[n % 2][:, 0:src.shape[1]], src).then_inc(slab_in[n % 2], 16)
                sp.dma_start(KFS[n % 2][:, :, :], KF[n]).then_inc(kfs_in[n % 2], 16)
            elif n > NF:
                sp.dma_start(SLAB[n % 2][:, :].rearrange("p (s t) -> p s t", s=2), A["inv_l"][n - NF - 1])\
                    .then_inc(slab_in[n % 2], 16)
            else:
                sp.dma_start(SLAB[n % 2][:, :].rearrange("p (f n) -> p f n", f=CB_),
                             A["inv_c"].rearrange("f p s t -> p f (s t)")).then_inc(slab_in[n % 2], 16)
        for m in range(2, KC):
            proj_load(A["ev_w_out"][0], m, plan["ev_out"].q + m)

        ffn("ffn1", A["ffn_w_in"][0, 1], A["ffn_w_out"][0, 1])
        ffn("ffn2", A["ffn_w_in"][1, 0], A["ffn_w_out"][1, 0])

        w_in = A["mla_w_in"][0].rearrange("(k p) n -> p k n", p=P)
        for n, at in enumerate(MLA_COLS):
            q = plan["mla_in"].q + n
            sp.wait_ge(lo_done, q - 1)
            w = min(P, w_in.shape[2] - at)
            sp.dma_start(RAW[raw_slot(q)][:, 0:KC * w].rearrange("p (k n) -> p k n", k=KC), w_in[:, :, at:at + w])\
                .then_inc(raw_in[raw_slot(q)], 16)
            if n == 1:
                sp.wait_ge(evac, plan["ln3"].evac)
                sp.dma_start(ROT[:, :], A["rope"]).then_inc(rot_in, 16)
        wq = A["mla_w_q_up"][0].rearrange("(k p) (h n) -> p k h n", p=P, h=MH)
        wkv = A["mla_w_kv_up"][0].rearrange("(k p) (h t n) -> p k h t n", p=P, h=MH, t=2)
        sp.wait_ge(pe["A"], plan["mla_out"].A)
        sp.wait_ge(pe["B"], plan["mla_out"].B)
        for k in range(KVC):
            sp.dma_start(VRAW[:, k, :].rearrange("p (h n) -> p h n", h=MH), wkv[:, k, :, 1, :]).then_inc(v_in, 16)

        def head_load(z, h):
            sp.dma_start(WRAW[z][:, 0:QC_ * QD].rearrange("p (k n) -> p k n", k=QC_),
                         wq[:, :, bass.ds(h, 1), :].squeeze(2)).then_inc(wr_in[z], 16)
            sp.dma_start(WRAW[z][:, QC_ * QD:].rearrange("p (k n) -> p k n", k=KVC),
                         wkv[:, :, bass.ds(h, 1), 0, :].squeeze(2)).then_inc(wr_in[z], 16)

        sp.wait_ge(v_pe, 2 * TB)
        for z in range(2):
            head_load(z, z)
        with sp.Fori(0, MH // 2 - 1) as i:
            for z in range(2):
                sp.wait_ge(wq_ok, 2 * i + z + 1)
                head_load(z, 2 * i + z + 2)
        for m in range(2):
            proj_load(A["mla_w_out"][0], m, plan["mla_out"].q + m)
        for z in range(2):
            sp.wait_ge(o_out[z], 16 * MH)
        for m in range(KC):
            sp.dma_start(OCH[:, m, :], OD[m * P:(m + 1) * P, :]).then_inc(och_in, 16)
        for m in range(2, KC):
            proj_load(A["mla_w_out"][0], m, plan["mla_out"].q + m)
        ffn("ffn3", A["ffn_w_in"][1, 1], A["ffn_w_out"][1, 1])
        for t in range(LAT // P):
            sp.wait_ge(fin_cp, 2 * (t + 1))
            sp.dma_start(out[0, t * P:(t + 1) * P, :], OUT[:, t, :]).then_inc(out_in, 16)
        sp.wait_ge(out_in, 16 * (LAT // P))

    @block.gpsimd
    def _(pool):
        pool.memset(ID[:, :], 0.0).then_inc(const_ok, 1)
        pool.memset(ONES[:, :], 1.0).then_inc(const_ok, 1)
        pool.memset(EPS[:, :], LN_EPS).then_inc(const_ok, 1)
        pool.memset(SC[:, :, :], 0.0).then_inc(const_ok, 1)
        pool.memset(ZERO[:, :], 0.0).then_inc(const_ok, 1)
        pool.wait_ge(const_ok, 5)
        pool.affine_select(out=ID[:, :], in_=ID[:, :], compare_op=ALU.not_equal, fill=1.0, base=0,
                           pattern=[[-1, P]], channel_multiplier=1).then_inc(const_ok, 1)

        def ada_loads(l, n0, group, i=0):
            for k in range(KC):
                slot = k % ADA_RING
                if not (isinstance(i, int) and KC * (n0 + i) + k < ADA_RING):
                    pool.wait_ge(ada_used, KC * n0 + k - ADA_RING + 1 + KC * i)
                src = A["ada_w"][l, k * P:(k + 1) * P, :].rearrange("p (g n) -> p g n", n=D)[
                    :, bass.ds(group, 1), :].squeeze(1)
                pool.dma_start(ADA[slot][:, :], src).then_inc(ada_in[slot], 16)

        for g in range(ADA_FIRST):
            ada_loads(0, g, g)
        with pool.Fori(0, N_ADA - ADA_FIRST) as i:
            ada_loads(0, plan["ffn0"].ada, i + ADA_FIRST, i)

        pool.wait_ge(evac, plan["ln0"].evac)
        for n in range(3):
            pool.memset(PAD[n][:, :], 0.0).then_inc(pad_zero, 1)
        pool.wait_ge(pe["A"], plan["ev_out"].A)
        pool.wait_ge(pe["B"], plan["ev_out"].B)
        for n in range(2):
            pool.memset(BD[n][:, :, :], 0.0).then_inc(bd_zero, 1)
        pool.wait_ge(bd_zero, 2)
        for n in range(2 * HC):
            c, d = n // 2, n % 2
            if n >= 2:
                pool.wait_ge(gate_pe, 2 * (n - 1))
            for v, w in enumerate((A["rg_a_w"], A["rg_x_w"])):
                for b in range(2):
                    pool.dma_start(BD[n % 2][64 * b:64 * b + 64, v, 64 * b:64 * b + 64], w[0, d, 2 * c + b])\
                        .then_inc(bd_in[n % 2], 16)

        pool.wait_ge(evac, plan["ln1"].evac)
        with pool.Fori(0, N_ADA) as i:
            ada_loads(1, plan["ffn1"].ada, i, i)

        def same(dst, src):
            zero = ZERO[0:src.shape[0], 0:1]
            for _ in src.shape[2:]:
                zero = zero.unsqueeze(1)
            return pool.tensor_tensor(dst, src, zero.broadcast_to(src.shape), ALU.add)

        def head_weights(i, d):
            z, h = d % 2, 2 * i + d
            pool.wait_ge(wr_in[z], 32 * (i + d // 2 + 1))
            if not isinstance(h, int) or h >= 2:
                pool.wait_ge(k_pe, 2 * (h - 1))
            q = WRAW[z][:, 0:QC_ * QD].rearrange("p (k n) -> p k n", k=QC_)
            swap = [(WRAW[z][:, 0:QC_ * QD].rearrange("p (k n) -> p k n", k=QC_)[:, :, NOPE:QD]
                     .rearrange("p k (a f j) -> p k a f j", a=2, f=2)[:, :, :, 1 - f, :],
                     lambda t, f=f: t[:, :, QD:P].rearrange("p k (a f j) -> p k a f j", a=2, f=2)[:, :, :, f, :])
                    for f in range(2)]
            parts = [(q, lambda t: t[:, :, 0:QD])] + swap
            k = WRAW[z][:, QC_ * QD:].rearrange("p (k n) -> p k n", k=KVC)
            todo = [(dst(WQH[z]), dst(WQL[z]), src) for src, dst in parts] + [(WKH[z][:, :, :], WKL[z][:, :, :], k)]
            for n, (hi, lo, src) in enumerate(todo):
                same(hi, src).then_inc(wq_hi, 1)
            pool.wait_ge(wq_hi, 4 * h + 4)
            for n, (hi, lo, src) in enumerate(todo):
                x = pool.tensor_tensor(lo, src, hi.bitcast(F32), ALU.subtract)
            x.then_inc(wq_ok, 1)

        def head_values(z, h):
            if not isinstance(h, int) or h >= 2:
                pool.wait_ge(av_pe, 2 * (h - 1))
            for src, dst in ((VH, VSH), (VL, VSL)):
                same(dst[z][:, :, :], src[:, :, :].bitcast(F32).rearrange("p t (h n) -> p t h n", h=MH)[
                    :, :, bass.ds(h, 1), :].squeeze(2)).then_inc(vs_ok, 1)

        def head_queries(z, h):
            pool.wait_ge(q_sum, h + 1)
            pool.wait_ge(q_cp, h + 1)
            if not isinstance(h, int) or h >= 2:
                pool.wait_ge(s_pe, QT_ * (h - 1))
            same(QH[z][0:QD, :], QT[0:QD, :]).then_inc(q_hi, 1)
            pool.wait_ge(q_hi, h + 1)
            pool.tensor_tensor(QLO[z][0:QD, :], QT[0:QD, :], QH[z][0:QD, :].bitcast(F32), ALU.subtract).then_inc(q_lo, 1)

        pool.wait_ge(v_tl, 2 * TB)
        pool.wait_ge(kr, 3)
        head_weights(0, 0)
        head_weights(0, 1)
        head_values(0, 0)
        head_queries(0, 0)

        def heads(i, last=False):
            for z in range(2):
                h = 2 * i + z
                if last and z == 1:
                    break
                head_queries(1 - z, h + 1)
                if not last:
                    head_weights(i, z + 2)
                head_values(1 - z, h + 1)
        heads(0)
        with pool.Fori(1, MH // 2 - 1) as i:
            heads(i)
        heads(MH // 2 - 1, last=True)

    @block.scalar
    def _(act):
        act.wait_ge(tr_taken, VT)
        lam = VEC["rg_lambda"][0]
        act.activation(SPL[:, 0, :], VECS[:, lam:lam + 2 * HC], ACT.Abs).then_inc(spl, 1)
        act.wait_ge(spl, 1)
        act.activation(SPL[:, 1, :], SPL[:, 0, :], ACT.Exp, scale=-1.0).then_inc(spl, 1)
        act.wait_ge(const_ok, 6)
        for n, name in enumerate(("c", "c_ctx")):
            at, rows = VEC[name]
            act.activation(SC[:, :, n], VECS[:, at:at + rows], ACT.Silu).then_inc(cond_ok, 1)

        def ada_take(n):
            act.wait_ge(ada_sum, n + 1)
            if not (isinstance(n, int) and n == 0):
                act.wait_ge(ada_tr, n)
            act.activation(ADAP[:, :], PS[3][:, 0:D // 4], ACT.Copy).then_inc(ada_row, 1)

        for n in range(2):
            act.wait_ge(f_dve, 8 * (n + 1))
            act.activation(FS[:, :], FZ[:, :], ACT.Sin).then_inc(f_sin, 1)

        def spectra_take(n):
            for v in range(2):
                act.wait_ge(f_pe, 2 + 2 * TB + 2 * n + v + 1)
                if n >= 2 and v == 0:
                    act.wait_ge(kf_out[n % 2], 16 * (n // 2))
                act.activation(KOUT[:, n % 2, v, :], PS[4 + 2 * (n % 2) + v][:, :], ACT.Copy).then_inc(f_spec, 1)
            act.wait_ge(f_spec, 2 * (n + 1))
            act.dma_start(KF[n], KOUT[:, n % 2, :, :]).then_inc(kf_out[n % 2], 16)

        for n in range(NF):
            spectra_take(n)
        for g in range(ADA_FIRST):
            ada_take(g)

        def h_make(j, s, m, e):
            lo, n = SEGS[s]
            if e >= 2:
                act.wait_ge(h_lo, e - 1)
            act.activation(H32[:, e % 2, 0:n], X[:, m, lo:lo + n], ACT.Identity, bias=CB[:, j, m, s:s + 1],
                           scale=CG[:, j, m, s:s + 1]).then_inc(ln_h32, 1)
            act.wait_ge(ln_h32, e + 1)
            act.activation(HHI[:, m, lo:lo + n], H32[:, e % 2, 0:n], ACT.Copy).then_inc(h_hi, 1)

        act.wait_ge(tr_taken, plan["ada_first"].tr)
        act.wait_ge(coef_ok, COEF_FIRST)
        for s in range(2):
            for m in range(KC):
                h_make(0, s, m, plan["h0"].h + KC * s + m)
        for n in range(2):
            act.wait_ge(kf_out[n], 16 * NF // 2)

        def split_hi(slot, half, q, i, wait_pe):
            act.wait_ge(raw_in[raw_slot(q)], raw_value(q, i))
            if wait_pe is not None:
                act.wait_ge(pe[slot], wait_pe)
            act.activation(WHI[slot][:, 1024 * half:1024 * half + 1024], RAW[raw_slot(q)][:, :],
                           ACT.Copy).then_inc(hi_done, 1)

        def ffn(name, S, ada):
            p = plan[name]
            used = {"A": (p.A, S), "B": (p.B, S), "W": (p.W, KC * S)}

            def free_value(slot, u):
                base, per = used[slot]
                if isinstance(u, int) and base + per * u == 0:
                    return None
                return base + per * u

            def silus(slot, i):
                b = 0 if slot == "A" else 3
                if slot == "A" and not (isinstance(i, int) and p.g + i == 0):
                    act.wait_ge(glo[slot], p.g + i)
                for s in range(S):
                    lo, n = SEGS[s]
                    src = PS[b][:, 0:LAT] if s == 0 else PS[b + 2][:, 0:CTX]
                    act.wait_ge(pe[slot], (p.A if slot == "A" else p.B) + S * i + s + 1)
                    act.activation(GM[slot][:, lo:lo + n], src, ACT.Silu).then_inc(silu[slot], 1)

            def body(i, first=False, last=False, ada=False):
                if not first:
                    silus("B", i - 1)
                for slot, d, half, j in ffn_halves(last)[:2]:
                    split_hi(slot, half, p.q + j, i, free_value(slot, i + d))
                silus("A", i)
                for slot, d, half, j in ffn_halves(last)[2:]:
                    if ada and slot == "W" and half == 0:
                        ada_take(p.ada + i - 1)
                    split_hi(slot, half, p.q + j, i, free_value(slot, i + d))

            body(0, first=True)
            if ada:
                with act.Fori(1, 1 + ada) as i:
                    body(i, ada=True)
            if 1 + ada < FI - 1:
                with act.Fori(1 + ada, FI - 1) as i:
                    body(i)
            body(FI - 1, last=True)
            silus("B", FI - 1)

        def first_unit(name):
            p = plan[name]
            for half in range(2):
                split_hi("A", half, p.q + half, 0, p.A if p.A else None)

        def layernorm(name, S, banks=(0, 3), j=0, last=False):
            p = plan[name]
            for s in range(S):
                lo, n = SEGS[s]
                act.wait_ge(ln_pe, 2 * p.ln + s + 1)
                act.activation(MU[:, lo:lo + n], PS[banks[s]][:, 0:n], ACT.Copy, scale=1.0 / D).then_inc(ln_mu, 1)
                for m in range(KC):
                    act.wait_ge(ln_cen, KC * (p.ln + s) + m + 1)
                    act.activation(SQ[:, m, lo:lo + n], X[:, m, lo:lo + n], ACT.Square).then_inc(ln_sq, 1)
            for s in range(S):
                lo, n = SEGS[s]
                act.wait_ge(ln_pe, 2 * p.ln + S + s + 1)
                act.activation(RSTD[:, lo:lo + n], PS[banks[s]][:, 0:n], ACT.Sqrt, bias=EPS[:, 0:1],
                               scale=1.0 / D).then_inc(ln_std, 1)
            for s in range(0 if last else S):
                for m in range(KC):
                    act.wait_ge(ln_n, KC * (p.ln + s) + m + 1)
                    h_make(j, s, m, p.h + s * KC + m)

        def even_mixer():
            p, po = plan["ev_in"], plan["ev_out"]

            def ev_split(name, u, per):
                b = plan[name]
                slot = "AB"[u % 2]
                for half in range(2):
                    split_hi(slot, half, b.q + 2 * u + half, 0, (b.A if slot == "A" else b.B) + per * (u // 2))

            ev_split("ev_in", 1, 3)
            pad = 0
            for u in range(10):
                if u + 2 < 10:
                    ev_split("ev_in", u + 2, 3)
                slot, b = "AB"[u % 2], 3 * (u % 2)
                base = (p.A if slot == "A" else p.B) + 3 * (u // 2)
                dst = []
                for half in range(2):
                    if u < HC and half == 1:
                        dst.append(None)
                    else:
                        dst.append(pad)
                        pad += 1
                if u == 0:
                    act.wait_ge(pad_zero, 3)
                for s in range(2):
                    for half in range(2):
                        act.wait_ge(pe[slot], base + (half + 1 if s == 0 else 3))
                        src = PS[b + half][:, 0:LAT] if s == 0 else PS[b + 2][:, CTX * half:CTX * half + CTX]
                        lo, n = GSEGS[s]
                        if dst[half] is None:
                            act.activation(GATED[:, u, lo:lo + n], src, ACT.Gelu_apprx_tanh).then_inc(mx_taken, 1)
                        else:
                            k = dst[half]
                            if k >= 3:
                                act.wait_ge(conv, CONV_END[k - 3])
                            act.activation(PAD[k % 3][:, LAG + lo:LAG + lo + n], src, ACT.Copy).then_inc(mx_taken, 1)

            for t in range(TB):
                act.wait_ge(ut_pe, t + 1)
                act.activation(UT[:, t, :], PS[4 + t % 4][:, :], ACT.Copy).then_inc(ut_ok, 1)

            def root(n):
                act.wait_ge(r_m, n + 1)
                act.activation(TH[n % 2][:, :], TH[n % 2][:, :], ACT.Sqrt).then_inc(r_sqrt, 1)

            ab, xb = VEC["rg_a_b"][0], VEC["rg_x_b"][0]
            for n in range(2 * HC):
                c, d = n // 2, n % 2
                col = HC * d + c
                for s in range(2):
                    lo, w = GSEGS[s]
                    act.wait_ge(gate_pe, 2 * n + s + 1)
                    if n >= 2 and s == 0:
                        act.wait_ge(r_scan, 2 * (n - 1))
                    if n == 0 and s == 0:
                        act.wait_ge(r_y, 1)
                    for v, (dst, bias) in enumerate(((RR, ab), (IG, xb))):
                        src = PS[v][:, 0:LAT] if s == 0 else PS[2][:, CTX * v:CTX * v + CTX]
                        act.activation(dst[n % 2][:, lo:lo + w], src, ACT.Sigmoid,
                                       bias=VECS[:, bias + col:bias + col + 1]).then_inc(r_sig, 1)
                act.wait_ge(r_sig, 4 * (n + 1))
                if n == 0:
                    act.wait_ge(spl, SPL_N)
                act.activation(AA[n % 2][:, :], RR[n % 2][:, :], ACT.Exp, scale=SPL[:, 6, col:col + 1]).then_inc(r_exp, 1)
                act.activation(TH[n % 2][:, :], RR[n % 2][:, :], ACT.Tanh, scale=SPL[:, 7, col:col + 1]).then_inc(r_tanh, 1)
                if n >= 1:
                    root(n - 1)
            root(2 * HC - 1)

            act.wait_ge(inv_pe, LB + HC)
            ev_split("ev_out", 0, 3)
            ev_split("ev_out", 1, 3)
            ev_split("ev_out", 2, 3)
            ev_split("ev_out", 3, 3)

        first_unit("ffn0")
        ffn("ffn0", 2, N_ADA - ADA_FIRST)
        first_unit("ev_in")
        layernorm("ln0", 2, j=1)
        even_mixer()
        first_unit("ffn1")
        layernorm("ln1", 2, (6, 7), j=2)
        ffn("ffn1", 2, N_ADA)
        first_unit("ffn2")
        layernorm("ln2", 2, j=3)
        ffn("ffn2", 2, 0)
        first_unit("mla_in")
        layernorm("ln3", 2, j=4)

        def odd_mixer():
            p = plan["mla_in"]

            def in_split(u):
                slot = "AB"[u % 2]
                base = (p.A, p.B)[u % 2]
                before = [0, 0, 3, 2, 5][u]
                for half in range(1 if u == 1 else 2):
                    q = p.q + MLA_HALF[u] + half
                    if u != 1:
                        split_hi(slot, half, q, 0, base + before)
                        continue
                    act.wait_ge(raw_in[raw_slot(q)], raw_value(q))
                    act.wait_ge(pe["B"], base)
                    for n, (src, dst) in enumerate(KR_PARTS(RAW[raw_slot(q)], WHI["B"])):
                        x = act.activation(dst, src, ACT.Copy)
                    x.then_inc(hi_done, 1)

            in_split(1)
            for u in range(5):
                slot, b = "AB"[u % 2], 3 * (u % 2)
                if u + 2 < 5:
                    in_split(u + 2)
                if u == 1:
                    act.wait_ge(pe["B"], p.B + 2)
                    act.activation(KRT[NOPE:QD, LAT:TOK], PS[5][0:ROPE, 0:CTX], ACT.Copy).then_inc(m_taken, 1)
                    continue
                for s in range(2 if u == 0 else 1):
                    lo, n = SEGS[s]
                    for half in range(2):
                        src = PS[b + half][:, 0:LAT] if s == 0 else PS[b + 2][:, CTX * half:CTX * half + CTX]
                        group = {0: (half + 1, 3), 2: (4 + half, 0), 3: (3 + half, 0), 4: (6 + half, 0)}[u][s]
                        act.wait_ge(pe[slot], (p.A, p.B)[u % 2] + group)
                        dst = KV[:, half, lo:lo + n] if u == 0 else QC[:, 2 * (u - 2) + half, :]
                        act.activation(dst, src, ACT.Copy).then_inc(m_taken, 1)

            for e, (T, chunks, lo, n, rs, width) in enumerate(RMS):
                act.wait_ge(m_taken, 5 if e < 2 else 11)
                if e:
                    act.wait_ge(mr_pe, e)
                for c in range(chunks):
                    act.activation(SQQ[:, c, 0:n], T[:, c, lo:lo + n], ACT.Square).then_inc(mr_sq, 1)
                act.wait_ge(mr_pe, e + 1)
                act.activation(rs[:, lo:lo + n], PS[6 + e % 2][:, 0:n], ACT.Sqrt, bias=EPS[:, 0:1], scale=1.0 / width)\
                    .then_inc(mr_std, 1)
            act.wait_ge(v_in, 16 * KVC)
            act.activation(WVH[:, :, :], VRAW[:, :, :], ACT.Copy).then_inc(v_hi, 1)
            for e, (T, chunks, lo, n, rs, width) in enumerate(RMS[:2]):
                for c in range(chunks):
                    act.wait_ge(mr_n, e * KVC + c + 1)
                    act.activation(KVH[:, c, lo:lo + n], T[:, c, lo:lo + n], ACT.Copy).then_inc(mr_hi, 1)
            for t in range(2 * TB):
                if 0 <= t - 2 < QC_:
                    act.wait_ge(mr_n, 2 * KVC + t - 1)
                    act.activation(QNH[:, t - 2, :], QC[:, t - 2, :], ACT.Copy).then_inc(mr_hi, 1)
                act.wait_ge(v_pe, t + 1)
                act.activation(VH[:, t // 2, 512 * (t % 2):512 * (t % 2) + 512], PS[t % 4][:, :], ACT.Copy).then_inc(v_th, 1)
            act.wait_ge(kr, 1)
            act.wait_ge(m_taken, 5)
            act.wait_ge(v_pe, 2 * TB)
            for z in range(2):
                act.activation(KH[z][NOPE:QD, :], KRT[NOPE:QD, :], ACT.Copy).then_inc(krp, 1)

            def proj_take(z, h, piece):
                if piece == 0:
                    act.wait_ge(q_pe, h + 1)
                    if not (isinstance(h, int) and h == 0):
                        act.wait_ge(q_lo, h)
                    act.activation(QT[0:NOPE, :], PS[7][0:NOPE, :], ACT.Copy).then_inc(q_cp, 1)
                else:
                    lo, n = SEGS[piece - 1]
                    act.wait_ge(k_pe, 2 * h + piece)
                    if not (isinstance(h, int) and h < 2):
                        act.wait_ge(s_pe, QT_ * (h - 1))
                    act.activation(KH[z][0:NOPE, lo:lo + n], PS[7][0:NOPE, 0:n], ACT.Copy).then_inc(k_hi, 1)

            def probs(g, s):
                act.wait_ge(s_nb, g + 1)
                if not (isinstance(g, int) and g < 2):
                    act.wait_ge(t_pe, g - 1)
                act.activation(PR[s % 2][:, :], SC_(s), ACT.Exp, bias=STAT[s % 2][:, 1:2], scale=SCALE,
                               accum_out=STAT[s % 2][:, 2:3]).then_inc(s_exp, 1)

            def turned(i, s):
                act.wait_ge(t_pe, 8 * i + s + 1)
                if not (isinstance(i, int) and 4 * i + s // 2 < 2):
                    act.wait_ge(av_pe, 4 * i + s // 2 - 1)
                act.activation(PTH[(s // 2) % 2][:, :, P * (s % 2):P * (s % 2) + P], TR_, ACT.Copy).then_inc(pt_hi, 1)

            def out_take(i, e):
                act.wait_ge(av_pe, 4 * i + e + 1)
                if not (isinstance(i, int) and 4 * i + e < 2):
                    act.wait_ge(o_out[e % 2], 16 * (2 * i + e // 2))
                act.activation(OS[e % 2][:, :], PS[6][0:VD, 0:CTX], ACT.Copy).then_inc(o_cp, 1)
                act.wait_ge(o_cp, 4 * i + e + 1)
                act.dma_start(OD.rearrange("(h d) (e t) -> h d e t", d=VD, e=2)[bass.ds(2 * i + e // 2, 1), :, e % 2, :]
                              .squeeze(0), OS[e % 2][:, :]).then_inc(o_out[e % 2], 16)

            def body(i, first=False, last=False):
                for s in range(2 * QT_):
                    g, z = 8 * i + s, s // QT_
                    if s % 4 > 0 and not (last and z == 1):
                        proj_take(1 - z, 2 * i + z + 1, s % 4 - 1)
                    probs(g, s)
                    if s % 2 == 0 and not (first and z == 0):
                        out_take(i, s // 2 - 2)
                    if not (first and s == 0):
                        turned(i, s - 1)

            for piece in range(3):
                proj_take(0, 0, piece)
            body(0, first=True)
            with act.Fori(1, MH // 2 - 1) as i:
                body(i)
            body(MH // 2 - 1, last=True)
            turned(MH // 2 - 1, 7)
            for e in (2, 3):
                out_take(MH // 2 - 1, e)

            act.wait_ge(och_in, 16 * KC)
            act.wait_ge(av_pe, 2 * MH)
            for m in range(KC):
                act.activation(HHI[:, m, 0:LAT], OCH[:, m, :], ACT.Copy).then_inc(och_hi, 1)
            b = plan["mla_out"]
            for u in range(4):
                for half in range(2):
                    split_hi("AB"[u % 2], half, b.q + 2 * u + half, 0, (b.A, b.B)[u % 2] + 2 * (u // 2))

        odd_mixer()
        first_unit("ffn3")
        layernorm("ln4", 1, (6,), j=5)
        ffn("ffn3", 1, 0)
        layernorm("final", 1, (0,), last=True)
        for t in range(LAT // P):
            for half in range(2):
                act.wait_ge(fin_tr, 2 * t + half + 1)
                act.activation(OUT[:, t, 512 * half:512 * half + 512], PS[2 + (2 * t + half) % 4][:, :], ACT.Copy).then_inc(fin_cp, 1)

    @block.vector
    def _(dve):
        dve.memset(AG[:, 0, :], ALPHA).then_inc(coef_ok, 1)
        dve.memset(AB[:, 0, :], 0.0).then_inc(coef_ok, 1)
        for t in range(VT):
            dve.wait_ge(tr_done, t + 1)
            dve.tensor_copy(VECS[:, t * P:(t + 1) * P], PS[t % 2][:, 0:P]).then_inc(tr_taken, 1)

        def x_take(m):
            tr = plan["x"].tr
            dve.wait_ge(tr_done, tr + 2 * m + 1)
            dve.tensor_copy(X[:, m, 0:LAT], PS[2 * (m % 2)][:, 0:LAT]).then_inc(tr_taken, 1)
            dve.wait_ge(tr_done, tr + 2 * m + 2)
            dve.tensor_copy(X[:, m, LAT:TOK], PS[2 * (m % 2) + 1][:, 0:CTX]).then_inc(tr_taken, 1)

        for m in range(KC):
            x_take(m)

        TURN = 2 * math.pi
        C1 = 6.28125
        C2 = float(np.array(np.array(TURN - C1, np.float32).view(np.uint32) & np.uint32(0xFFFFF000), np.uint32).view(np.float32))
        C3 = TURN - C1 - C2
        MAGIC = 1.5 * 2.0 ** 23
        PI = float(np.nextafter(np.float32(math.pi), np.float32(0)))
        nf = [0]

        def fl(ins):
            nf[0] += 1
            ins.then_inc(f_dve, 1)
            dve.wait_ge(f_dve, nf[0])

        dve.wait_ge(flt_in, 16 * 8)
        for n in range(2):
            dve.wait_ge(f_pe, n + 1)
            for s in range(2):
                lo, w = SEGS[s]
                fl(dve.tensor_scalar(FZ[:, lo:lo + w], PS[4 + s][0:FH, 0:w], FVEC[:, n:n + 1], FVEC[:, 2 + n:3 + n],
                                     ALU.add, ALU.mult))
            fl(dve.tensor_scalar(FN[:, :], FZ[:, :], 1.0 / TURN, MAGIC, ALU.mult, ALU.add))
            fl(dve.tensor_scalar(FN[:, :], FN[:, :], -MAGIC, None, ALU.add))
            for cst in (C1, C2, C3):
                fl(dve.scalar_tensor_tensor(FZ[:, :], FN[:, :], -cst, FZ[:, :], ALU.mult, ALU.add))
            fl(dve.tensor_scalar(FZ[:, :], FZ[:, :], -PI, PI, ALU.max, ALU.min))
        dve.wait_ge(tab_in, 16 * 7)
        for t in range(TB):
            dve.wait_ge(f_pe, 2 + 2 * (t + 1))
            if t:
                dve.wait_ge(f_filt, 2 * t)
            for v in range(2):
                dve.tensor_tensor(HF_[:, v, :], PS[4 + 2 * (t % 2) + v][:, :], WINT[:, t, v, :], ALU.mult).then_inc(f_win, 1)
            dve.wait_ge(f_win, 2 * (t + 1))
            dve.tensor_tensor(FILT[:, t, 0, :], HF_[:, 1, :], HF_[:, 0, :], ALU.add).then_inc(f_filt, 1)
            dve.tensor_tensor(FILT[:, t, 1, :], HF_[:, 1, :], HF_[:, 0, :], ALU.subtract).then_inc(f_filt, 1)

        ns = [2]

        def sl(ins):
            ns[0] += 1
            ins.then_inc(spl, 1)
            dve.wait_ge(spl, ns[0])

        dve.wait_ge(spl, 2)
        sl(dve.tensor_scalar(SPL[:, 2, :], SPL[:, 1, :], 2.0, None, ALU.add))
        sl(dve.reciprocal(SPL[:, 3, :], SPL[:, 2, :]))
        sl(dve.tensor_tensor(SPL[:, 2, :], SPL[:, 1, :], SPL[:, 3, :], ALU.mult))
        sl(dve.tensor_tensor(SPL[:, 3, :], SPL[:, 2, :], SPL[:, 2, :], ALU.mult))
        sl(dve.tensor_scalar(SPL[:, 4, :], SPL[:, 3, :], 1.0 / 17, 1.0 / 15, ALU.mult, ALU.add))
        for o in (13, 11, 9, 7, 5, 3, 1):
            sl(dve.tensor_tensor(SPL[:, 4, :], SPL[:, 4, :], SPL[:, 3, :], ALU.mult))
            sl(dve.tensor_scalar(SPL[:, 4, :], SPL[:, 4, :], 1.0 / o, None, ALU.add))
        sl(dve.tensor_tensor(SPL[:, 4, :], SPL[:, 4, :], SPL[:, 2, :], ALU.mult))
        sl(dve.tensor_scalar(SPL[:, 5, :], VECS[:, VEC["rg_lambda"][0]:VEC["rg_lambda"][0] + 2 * HC], -1.0, 0.0, ALU.mult, ALU.max))
        sl(dve.scalar_tensor_tensor(SPL[:, 5, :], SPL[:, 4, :], 2.0, SPL[:, 5, :], ALU.mult, ALU.add))
        sl(dve.tensor_scalar(SPL[:, 6, :], SPL[:, 5, :], -8.0, None, ALU.mult))
        sl(dve.tensor_scalar(SPL[:, 7, :], SPL[:, 5, :], 8.0, None, ALU.mult))
        assert ns[0] == SPL_N

        def mod_take(n, t):
            dve.wait_ge(ada_tr, n + 1)
            at = VEC["ada_b"][0]
            dve.tensor_tensor(
                MOD[:, bass.ds(KC * t, KC), :].rearrange("p (j q) v -> p j q v", q=2),
                PS[4][:, 0:2 * P].rearrange("p (q j c) -> p j q c", q=2, j=4)[:, :, :, 0:2],
                VECS[:, bass.ds(at + KC * t, KC)].rearrange("p (j q) -> p j q", q=2).unsqueeze(3).broadcast_to([P, 4, 2, 2]),
                ALU.add).then_inc(mod_ok, 1)

        for g in range(ADA_FIRST):
            mod_take(g, g)

        nco = [2]

        def co(ins):
            nco[0] += 1
            ins.then_inc(coef_ok, 1)

        def co_wait():
            dve.wait_ge(coef_ok, nco[0])

        def coefs(j, shift, ln=None):
            sh = MOD[:, KC * shift:KC * shift + KC, :]
            sc = MOD[:, KC * shift + KC:KC * shift + 2 * KC, :]
            if ln is None:
                co(dve.tensor_scalar(CG[:, j, :, :], sc, 1.0, None, ALU.add))
                co(dve.tensor_copy(CB[:, j, :, :], sh))
                return
            g = VECS[:, VEC["ln_g"][0] + KC * ln:VEC["ln_g"][0] + KC * ln + KC]
            b = VECS[:, VEC["ln_b"][0] + KC * ln:VEC["ln_b"][0] + KC * ln + KC]
            g2, b2 = (v.unsqueeze(2).broadcast_to([P, KC, 2]) for v in (g, b))
            co(dve.tensor_scalar(CG[:, j, :, :], sc, 1.0, None, ALU.add))
            co_wait()
            co(dve.tensor_tensor(CB[:, j, :, :], CG[:, j, :, :], b2, ALU.mult))
            co_wait()
            co(dve.tensor_tensor(CB[:, j, :, :], CB[:, j, :, :], sh, ALU.add))
            co(dve.tensor_tensor(CG[:, j, :, :], CG[:, j, :, :], g2, ALU.mult))
            co(dve.tensor_scalar(AG[:, j, :], g, ALPHA, None, ALU.mult))
            co(dve.tensor_scalar(AB[:, j, :], b, ALPHA, None, ALU.mult))

        def gate(l, j):
            src = MOD[:, KC * (N_ADA * l + 3 * j + 2):KC * (N_ADA * l + 3 * j + 2) + KC, :]
            co(dve.tensor_scalar(GATE[:, 3 * l + j, :, :], src, 1.0 if j == 1 else 0.5, None, ALU.mult))

        dve.wait_ge(mod_ok, ADA_FIRST)
        coefs(0, 0)
        gate(0, 0)
        co_wait()

        def low_parts(s, e0, ready):
            lo, n = SEGS[s]
            ready(0)
            for m in range(KC):
                e = e0 + m
                if m + 1 < KC:
                    ready(m + 1)
                dve.wait_ge(h_hi, e + 1)
                dve.tensor_tensor(HLO[:, m, lo:lo + n], H32[:, e % 2, 0:n],
                                  HHI[:, m, lo:lo + n].bitcast(F32), ALU.subtract).then_inc(h_lo, 1)

        def residual(name, S, j):
            for s in range(S):
                lo, n = SEGS[s]
                for m in range(KC):
                    dve.wait_ge(ln_h32, plan[name].h + KC * s + m + 1)
                    dve.tensor_scalar(X[:, m, lo:lo + n], X[:, m, lo:lo + n], AG[:, j, m:m + 1],
                                      AB[:, j, m:m + 1], ALU.mult, ALU.add).then_inc(ln_x, 1)

        def first_unit(name):
            for half in range(2):
                split_lo("A", half, plan[name].q + half, 0)

        assert nco[0] == COEF_FIRST
        for s in range(2):
            low_parts(s, plan["h0"].h + KC * s, lambda m: None)

        def split_lo(slot, half, q, i):
            dve.wait_ge(hi_done, q + 1 + 6 * i)
            cols = slice(1024 * half, 1024 * half + 1024)
            dve.tensor_tensor(WLO[slot][:, cols], RAW[raw_slot(q)][:, :], WHI[slot][:, cols].bitcast(F32),
                              ALU.subtract).then_inc(lo_done, 1)

        def ffn(name, S, j, ada, t0, then):
            p = plan[name]

            def gated(slot, i):
                b = 0 if slot == "A" else 3
                for s in range(S):
                    lo, n = SEGS[s]
                    src = PS[b + 1][:, 0:LAT] if s == 0 else PS[b + 2][:, CTX:2 * CTX]
                    dve.wait_ge(silu[slot], p.gs + S * i + s + 1)
                    dve.tensor_tensor(GM[slot][:, lo:lo + n], GM[slot][:, lo:lo + n], src,
                                      ALU.mult).then_inc(mul[slot], 1)

            def parts(slot, i):
                T = TOK if S == 2 else LAT
                dve.wait_ge(mul[slot], p.gs + S * (i + 1))
                if slot == "A" and not (isinstance(i, int) and p.W + i == 0):
                    dve.wait_ge(pe["W"], p.W + KC * S * i)
                dve.tensor_copy(GHI[slot][:, 0:T], GM[slot][:, 0:T]).then_inc(ghi[slot], 1)
                dve.wait_ge(ghi[slot], p.g + i + 1)
                dve.tensor_tensor(GLO[slot][:, 0:T], GM[slot][:, 0:T], GHI[slot][:, 0:T].bitcast(F32),
                                  ALU.subtract).then_inc(glo[slot], 1)

            def accumulate(i, e):
                m, s = down_groups(S)[e]
                lo, n = SEGS[s]
                dve.wait_ge(pe["W"], p.W + KC * S * i + e + 1 + (s == 1 and m % 2 == 0))
                if S == 1 and not (isinstance(i, int) and i == 0):
                    dve.wait_ge(evac, p.evac + KC * S * (i - 1) + e + 1)
                dve.scalar_tensor_tensor(X[:, m, lo:lo + n], down_bank(m, s), GATE[:, j, m, s:s + 1],
                                         X[:, m, lo:lo + n], ALU.mult, ALU.add).then_inc(evac, 1)

            dve.wait_ge(ln_x, p.h)

            def body(i, first=False, last=False, ada=False):
                if not first:
                    gated("B", i - 1)
                    parts("B", i - 1)
                todo = [(slot, half, p.q + q) for slot, d, half, q in ffn_halves(last)]
                for _ in range(2):
                    split_lo(*todo.pop(0), i)
                gated("A", i)
                if not first:
                    for e in range(KC * S):
                        if e in (0, 2 * S) and todo and not last:
                            split_lo(*todo.pop(0), i)
                        if e == 12 and ada:
                            mod_take(p.ada + i - 1, t0 + i - 1)
                        accumulate(i - 1, e)
                parts("A", i)
                while todo:
                    split_lo(*todo.pop(0), i)

            body(0, first=True)
            if ada:
                with dve.Fori(1, 1 + ada) as i:
                    body(i, ada=True)
            if 1 + ada < FI - 1:
                with dve.Fori(1 + ada, FI - 1) as i:
                    body(i)
            body(FI - 1, last=True)
            gated("B", FI - 1)
            parts("B", FI - 1)
            if then:
                first_unit(then)
            for e in range(KC * S):
                accumulate(FI - 1, e)

        first_unit("ffn0")
        residual("h0", 2, 0)
        ffn("ffn0", 2, 0, N_ADA - ADA_FIRST, ADA_FIRST, "ev_in")

        dve.wait_ge(mod_ok, N_ADA)
        coefs(1, 3, 0)
        coefs(2, 6, 1)
        gate(0, 1)
        gate(0, 2)
        co_wait()

        def layernorm(name, S, j):
            p = plan[name]
            for s in range(S):
                lo, n = SEGS[s]
                dve.wait_ge(ln_mu, p.ln + s + 1)
                for m in range(KC):
                    dve.tensor_tensor(X[:, m, lo:lo + n], X[:, m, lo:lo + n], MU[:, lo:lo + n],
                                      ALU.subtract).then_inc(ln_cen, 1)
            for s in range(S):
                lo, n = SEGS[s]
                dve.wait_ge(ln_std, p.ln + s + 1)
                dve.reciprocal(RSTD[:, lo:lo + n], RSTD[:, lo:lo + n]).then_inc(ln_rstd, 1)
                dve.wait_ge(ln_rstd, p.ln + s + 1)
                dve.wait_ge(ln_sq, KC * (p.ln + s + 1))

                def ready(m):
                    dve.tensor_tensor(X[:, m, lo:lo + n], X[:, m, lo:lo + n], RSTD[:, lo:lo + n],
                                      ALU.mult).then_inc(ln_n, 1)
                if name == "final":
                    for m in range(KC):
                        ready(m)
                    for m in range(KC):
                        dve.wait_ge(ln_n, KC * (p.ln + s) + m + 1)
                        row = KC * (DEPTH * 3 - 1) + m
                        dve.tensor_scalar(X[:, m, lo:lo + n], X[:, m, lo:lo + n],
                                          VECS[:, VEC["ln_g"][0] + row:VEC["ln_g"][0] + row + 1],
                                          VECS[:, VEC["ln_b"][0] + row:VEC["ln_b"][0] + row + 1],
                                          ALU.mult, ALU.add).then_inc(fin_x, 1)
                    continue
                low_parts(s, p.h + KC * s, ready)

        def even_mixer():
            p, po = plan["ev_in"], plan["ev_out"]

            def ev_split(name, u):
                for half in range(2):
                    split_lo("AB"[u % 2], half, plan[name].q + 2 * u + half, 0)

            nc_ = [0]

            def step(ins, wait=True):
                nc_[0] += 1
                ins.then_inc(conv, 1)
                if wait:
                    dve.wait_ge(conv, nc_[0])

            def convolve(k, dst):
                kind, c = CONVS[k]
                taps, at, n, bias = ((4, VEC["rg_conv_w"][0], HC, VEC["rg_conv_b"][0]) if kind == "rg" else
                                     (3, VEC["hy_conv_w"][0], 3 * HC, VEC["hy_conv_b"][0]))
                first = 0 if kind == "rg" else 1
                for t in range(taps):
                    src = PAD[k % 3][:, first + t:first + t + GT_]
                    w = VECS[:, at + n * t + c:at + n * t + c + 1]
                    if t == 0:
                        step(dve.tensor_scalar(dst, src, w, VECS[:, bias + c:bias + c + 1], ALU.mult, ALU.add))
                    else:
                        step(dve.scalar_tensor_tensor(dst, src, w, dst, ALU.mult, ALU.add))

            ev_split("ev_in", 1)
            residual("ln0", 2, 1)
            for n in range(2):
                for t in (RR, IG, HS):
                    dve.memset(t[n][:, LAT:LAT + GAP], 0.0).then_inc(r_y, 1) if t is not HS or n == 0 else None
            for c in range(HC):
                dve.memset(GATED[:, c, LAT:LAT + GAP], 0.0).then_inc(r_y, 1)
            k = 0
            for u in range(10):
                if u + 2 < 10:
                    ev_split("ev_in", u + 2)
                for half in range(1 if u < HC else 2):
                    dve.wait_ge(mx_taken, 4 * u + 3 + half)
                    kind, c = CONVS[k]
                    if kind == "rg":
                        convolve(k, XC[:, c, :])
                    elif c < HC:
                        convolve(k, X0[:, c, :])
                    elif c < 2 * HC:
                        convolve(k, AA[0][:, :])
                    else:
                        convolve(k, AA[1][:, :])
                        step(dve.tensor_tensor(U[:, c - 2 * HC, :], AA[0][:, :], AA[1][:, :], ALU.mult))
                    assert nc_[0] == CONV_END[k]
                    k += 1
            dve.memset(HS[1][:, LAT:LAT + GAP], 0.0).then_inc(r_y, 1)
            RY0 = 2 + 2 + 1 + HC + 1

            def decay(n):
                c = n // 2
                dve.wait_ge(r_sig, 4 * (n + 1))
                dve.tensor_tensor(IG[n % 2][:, :], IG[n % 2][:, :], XC[:, c, :], ALU.mult).then_inc(r_in, 1)
                dve.wait_ge(r_exp, n + 1)
                dve.wait_ge(r_tanh, n + 1)
                dve.tensor_tensor(RR[n % 2][:, :], AA[n % 2][:, :], AA[n % 2][:, :], ALU.mult).then_inc(r_sq, 1)
                dve.wait_ge(r_sq, n + 1)
                dve.scalar_tensor_tensor(TH[n % 2][:, :], RR[n % 2][:, :], 1.0, TH[n % 2][:, :], ALU.add,
                                         ALU.mult).then_inc(r_m, 1)

            ny = [RY0]

            def ystep(ins):
                ny[0] += 1
                ins.then_inc(r_y, 1)
                dve.wait_ge(r_y, ny[0])

            def recur(n):
                c, d = n // 2, n % 2
                dve.wait_ge(r_sqrt, n + 1)
                dve.wait_ge(r_in, n + 1)
                dve.tensor_tensor(IG[n % 2][:, :], IG[n % 2][:, :], TH[n % 2][:, :], ALU.mult).then_inc(r_b, 1)
                dve.wait_ge(r_b, n + 1)
                (l0, ln), (c0, cn) = GSEGS
                lat, ctx = (slice(l0, l0 + ln), slice(c0, c0 + cn)) if d == 0 else (
                    slice(l0 + ln - 1, None, -1), slice(c0 + cn - 1, c0 - 1, -1))
                end = c0 + cn - 1 if d == 0 else c0
                a, b, h = AA[n % 2], IG[n % 2], HS[d]
                dve.tensor_tensor_scan(h[:, ctx], a[:, ctx], b[:, ctx], 0.0, ALU.mult, ALU.add).then_inc(r_scan, 1)
                dve.wait_ge(r_scan, 2 * n + 1)
                dve.tensor_tensor_scan(h[:, lat], a[:, lat], b[:, lat], h[:, end:end + 1], ALU.mult, ALU.add).then_inc(r_scan, 1)
                dve.wait_ge(r_scan, 2 * n + 2)
                if d == 0:
                    return
                ystep(dve.tensor_tensor(HS[0][:, :], HS[0][:, :], HS[1][:, :], ALU.add))
                ystep(dve.tensor_tensor(HS[0][:, :], HS[0][:, :], GATED[:, c, :], ALU.mult))
                for (lo, w), (g0, _) in zip(SEGS, GSEGS):
                    ystep(dve.tensor_copy(HHI[:, HC + c, lo:lo + w], HS[0][:, g0:g0 + w]))
                    dve.tensor_tensor(HLO[:, HC + c, lo:lo + w], HS[0][:, g0:g0 + w],
                                      HHI[:, HC + c, lo:lo + w].bitcast(F32), ALU.subtract).then_inc(y_rg, 1)
                dve.wait_ge(y_rg, 2 * c + 2)

            def spectrum(n):
                k, b = FREQ[n]
                yr, yq = (YL[:, 0, b, :], YL[:, 1, b, :]) if k == 0 else (YC[0][:, b, :], YC[1][:, b, :])
                pa, pb = PS[4 + 2 * (n % 2)][:, :], PS[5 + 2 * (n % 2)][:, :]
                kp, kq = KFS[n % 2][:, 0, :], KFS[n % 2][:, 1, :]
                dve.wait_ge(df_pe, n + 1)
                dve.wait_ge(kfs_in[n % 2], 16 * (n // 2 + 1))
                if n:
                    dve.wait_ge(df_y, 4 * n)
                dve.tensor_tensor(yr, pa, kp, ALU.mult).then_inc(hy_t, 1)
                dve.tensor_tensor(TMP[0][:, :], pb, kq, ALU.mult).then_inc(df_y, 1)
                dve.tensor_tensor(yq, pb, kp, ALU.mult).then_inc(hy_t, 1)
                dve.tensor_tensor(TMP[1][:, :], pa, kq, ALU.mult).then_inc(df_y, 1)
                dve.wait_ge(hy_t, 2 * n + 2)
                dve.wait_ge(df_y, 4 * n + 2)
                dve.tensor_tensor(yr, yr, TMP[0][:, :], ALU.add).then_inc(df_y, 1)
                dve.tensor_tensor(yq, yq, TMP[1][:, :], ALU.subtract).then_inc(df_y, 1)

            for n in range(2 * HC):
                decay(n)
                if n:
                    recur(n - 1)
                    if n - 1 < NF:
                        spectrum(n - 1)
            recur(2 * HC - 1)

            nh = [2 * NF]

            def hstep(ins):
                nh[0] += 1
                ins.then_inc(hy_t, 1)
                dve.wait_ge(hy_t, nh[0])

            def hy_output(s, c):
                (lo, w), (g0, _) = SEGS[s], GSEGS[s]
                src = PS[4 + c][:, 0:LAT] if s == 0 else PS[c // 2][:, CTX * (c % 2):CTX * (c % 2) + CTX]
                t, u = X0[:, c, g0:g0 + w], U[:, c, g0:g0 + w]
                hb = VEC["hy_bias"][0] + c
                hstep(dve.scalar_tensor_tensor(u, u, VECS[:, hb:hb + 1], src, ALU.mult, ALU.add))
                hstep(dve.tensor_tensor(t, t, u, ALU.mult))

            def hy_parts(s, c):
                (lo, w), (g0, _) = SEGS[s], GSEGS[s]
                t = X0[:, c, g0:g0 + w]
                hstep(dve.tensor_copy(HHI[:, c, lo:lo + w], t))
                dve.tensor_tensor(HLO[:, c, lo:lo + w], t, HHI[:, c, lo:lo + w].bitcast(F32),
                                  ALU.subtract).then_inc(y_hy, 1)

            dve.wait_ge(inv_pe, HC)
            for c in range(HC):
                hy_output(1, c)
            dve.wait_ge(inv_pe, LB + HC)
            ev_split("ev_out", 0)
            for c in range(HC):
                hy_output(0, c)
                hy_parts(0, c)
            for c in range(HC):
                hy_parts(1, c)
            ev_split("ev_out", 1)
            proj_accumulate("ev_out", 2, 1, "ffn1")

        def proj_accumulate(name, S, j, then):
            b = plan[name]
            for u in range(4):
                slot, k = "AB"[u % 2], 3 * (u % 2)
                base = (b.A if slot == "A" else b.B) + (S + 1) * (u // 2)
                if u == 3:
                    first_unit(then)
                for s in range(S):
                    lo, w = SEGS[s]
                    for half in range(2):
                        m = 2 * u + half
                        dve.wait_ge(pe[slot], base + (half + 1 if s == 0 else 3))
                        src = PS[k + half][:, 0:LAT] if s == 0 else PS[k + 2][:, CTX * half:CTX * half + CTX]
                        dve.scalar_tensor_tensor(X[:, m, lo:lo + w], src, GATE[:, j, m, s:s + 1], X[:, m, lo:lo + w],
                                                 ALU.mult, ALU.add).then_inc(evac, 1)
                if u + 2 < 4:
                    for half in range(2):
                        split_lo(slot, half, b.q + 2 * (u + 2) + half, 0)

        layernorm("ln0", 2, 1)
        even_mixer()
        layernorm("ln1", 2, 2)
        residual("ln1", 2, 2)
        ffn("ffn1", 2, 2, N_ADA, N_ADA, "ffn2")
        dve.wait_ge(mod_ok, DEPTH * N_ADA)
        coefs(3, N_ADA, 2)
        coefs(4, N_ADA + 3, 3)
        coefs(5, N_ADA + 6, 4)
        for j in range(3):
            gate(1, j)
        co_wait()
        layernorm("ln2", 2, 3)
        residual("ln2", 2, 3)
        ffn("ffn2", 2, 3, 0, 0, "mla_in")
        layernorm("ln3", 2, 4)

        def odd_mixer():
            p = plan["mla_in"]

            def in_split(u):
                slot = "AB"[u % 2]
                for half in range(1 if u == 1 else 2):
                    q = p.q + MLA_HALF[u] + half
                    if u != 1:
                        split_lo(slot, half, q, 0)
                        continue
                    dve.wait_ge(hi_done, q + 1)
                    for (src, hi), (_, lo) in zip(KR_PARTS(RAW[raw_slot(q)], WHI["B"]), KR_PARTS(RAW[raw_slot(q)], WLO["B"])):
                        x = dve.tensor_tensor(lo, src, hi.bitcast(F32), ALU.subtract)
                    x.then_inc(lo_done, 1)

            in_split(1)
            in_split(2)
            residual("ln3", 2, 4)
            dve.wait_ge(rot_in, 16)
            dve.wait_ge(pe["B"], p.B + 1)
            dve.tensor_tensor(KRT[NOPE:QD, 0:LAT], PS[3][0:ROPE, :], ROT[0:ROPE, :], ALU.mult).then_inc(krp, 1)
            dve.tensor_tensor(KR2[NOPE:QD, :], PS[3][ROPE:2 * ROPE, :], ROT[ROPE:2 * ROPE, :], ALU.mult).then_inc(krp, 1)
            in_split(3)
            in_split(4)
            dve.wait_ge(krp, 2)
            dve.tensor_tensor(KRT[NOPE:QD, 0:LAT], KRT[NOPE:QD, 0:LAT], KR2[NOPE:QD, :], ALU.add).then_inc(kr, 1)

            qn, kvn = VEC["mla_q_norm"][0], VEC["mla_kv_norm"][0]

            def rms_scale(e):
                T, chunks, lo, n, rs, width = RMS[e]
                dve.wait_ge(mr_std, e + 1)
                dve.reciprocal(rs[:, lo:lo + n], rs[:, lo:lo + n]).then_inc(mr_rs, 1)
                dve.wait_ge(mr_rs, e + 1)

            def rms_norm(e, c):
                T, chunks, lo, n, rs, width = RMS[e]
                g = VECS[:, (kvn if e < 2 else qn) + c:(kvn if e < 2 else qn) + c + 1]
                dve.scalar_tensor_tensor(T[:, c, lo:lo + n], T[:, c, lo:lo + n], g, rs[:, lo:lo + n],
                                         ALU.mult, ALU.mult).then_inc(mr_n, 1)

            def rms_low(e, c):
                T, chunks, lo, n, rs, width = RMS[e]
                dve.wait_ge(mr_hi, e * KVC + c + 1)
                dst, hi = (KVL_[:, c, lo:lo + n], KVH[:, c, lo:lo + n]) if e < 2 else (QNL[:, c, :], QNH[:, c, :])
                dve.tensor_tensor(dst, T[:, c, lo:lo + n], hi.bitcast(F32), ALU.subtract).then_inc(mr_lo, 1)

            for e in range(2):
                rms_scale(e)
                for c in range(KVC):
                    rms_norm(e, c)
            dve.wait_ge(v_hi, 1)
            dve.tensor_tensor(WVL[:, :, :], VRAW[:, :, :], WVH[:, :, :].bitcast(F32), ALU.subtract).then_inc(v_lo, 1)
            for e in range(2):
                for c in range(KVC):
                    rms_low(e, c)
            rms_scale(2)
            for t in range(2 * TB):
                if t < QC_:
                    rms_norm(2, t)
                if 0 <= t - 3 < QC_:
                    rms_low(2, t - 3)
                cols = slice(512 * (t % 2), 512 * (t % 2) + 512)
                dve.wait_ge(v_th, t + 1)
                dve.tensor_tensor(VL[:, t // 2, cols], PS[t % 4][:, :], VH[:, t // 2, cols].bitcast(F32),
                                  ALU.subtract).then_inc(v_tl, 1)
            for z in range(2):
                dve.wait_ge(krp, 3 + z)
                dve.tensor_tensor(KLO[z][NOPE:QD, :], KRT[NOPE:QD, :], KH[z][NOPE:QD, :].bitcast(F32),
                                  ALU.subtract).then_inc(kr, 1)

            def proj_part(z, h, piece):
                if piece == 0:
                    dve.wait_ge(q_pe, h + 1)
                    if not (isinstance(h, int) and h == 0):
                        dve.wait_ge(q_lo, h)
                    dve.tensor_tensor(QT[NOPE:QD, :], PS[7][NOPE:QD, :], ROT[NOPE:QD, :], ALU.mult).then_inc(q_rot, 1)
                    dve.tensor_tensor(QR2[NOPE:QD, :], PS[7][QD:P, :], ROT[QD:P, :], ALU.mult).then_inc(q_rot, 1)
                    dve.wait_ge(q_rot, 2 * h + 2)
                    dve.tensor_tensor(QT[NOPE:QD, :], QT[NOPE:QD, :], QR2[NOPE:QD, :], ALU.add).then_inc(q_sum, 1)
                else:
                    lo, n = SEGS[piece - 1]
                    dve.wait_ge(k_hi, 2 * h + piece)
                    dve.tensor_tensor(KLO[z][0:NOPE, lo:lo + n], PS[7][0:NOPE, 0:n], KH[z][0:NOPE, lo:lo + n].bitcast(F32),
                                      ALU.subtract).then_inc(k_lo, 1)

            def turned(i, s):
                dve.wait_ge(pt_hi, 8 * i + s + 1)
                at = slice(P * (s % 2), P * (s % 2) + P)
                dve.tensor_tensor(PTL[(s // 2) % 2][:, :, at], TR_, PTH[(s // 2) % 2][:, :, at].bitcast(F32),
                                  ALU.subtract).then_inc(pt_lo, 1)

            def body(i, first=False, last=False):
                for s in range(2 * QT_):
                    g, z = 8 * i + s, s // QT_
                    st = STAT[s % 2]
                    dve.wait_ge(s_pe, g + 1)
                    if not (isinstance(g, int) and g < 2):
                        dve.wait_ge(s_norm, g - 1)
                    dve.tensor_reduce(st[:, 0:1], SC_(s), mybir.AxisListType.X, ALU.max).then_inc(s_max, 1)
                    dve.wait_ge(s_max, g + 1)
                    dve.tensor_scalar(st[:, 1:2], st[:, 0:1], -SCALE, None, ALU.mult).then_inc(s_nb, 1)
                    if s % 4 > 0 and not (last and z == 1):
                        proj_part(1 - z, 2 * i + z + 1, s % 4 - 1)
                    dve.wait_ge(s_exp, g + 1)
                    dve.reciprocal(st[:, 3:4], st[:, 2:3]).then_inc(s_inv, 1)
                    dve.wait_ge(s_inv, g + 1)
                    dve.tensor_scalar(DIAG[s % 2][:, :], ID[:, :], st[:, 3:4], None, ALU.mult).then_inc(s_norm, 1)
                    if not (first and s == 0):
                        turned(i, s - 1)

            for piece in range(3):
                proj_part(0, 0, piece)
            body(0, first=True)
            with dve.Fori(1, MH // 2 - 1) as i:
                body(i)
            body(MH // 2 - 1, last=True)
            turned(MH // 2 - 1, 7)

            b = plan["mla_out"]
            for m in range(KC):
                dve.wait_ge(och_hi, m + 1)
                dve.tensor_tensor(HLO[:, m, 0:LAT], OCH[:, m, :], HHI[:, m, 0:LAT].bitcast(F32), ALU.subtract).then_inc(och_lo, 1)
                if m < 4:
                    split_lo("AB"[m // 2], m % 2, b.q + m, 0)
            proj_accumulate("mla_out", 1, 4, "ffn3")

        odd_mixer()
        layernorm("ln4", 1, 5)
        residual("ln4", 1, 5)
        ffn("ffn3", 1, 5, 0, 0, None)
        layernorm("final", 1, 6)

    @block.tensor
    def _(te):
        te.wait_ge(const_ok, 6)
        te.wait_ge(vin_in, 16 * len(vec_pieces()))
        for t in range(VT):
            if t >= 2:
                te.wait_ge(tr_taken, t - 1)
            r = min(P, VROWS - t * P)
            te.transpose(PS[t % 2][:, 0:r], VIN[0:r, t, :], ID[0:r, 0:r]).then_inc(tr_done, 1)
        te.wait_ge(xin_in, 16 * TOK // P)
        for m in range(KC):
            for s in range(2):
                lo, n = SEGS[s]
                e = plan["x"].tr + 2 * m + s
                te.wait_ge(tr_taken, e - 3 if m >= 2 else VT)
                for t in range(n // P):
                    x = te.transpose(PS[2 * (m % 2) + s][:, t * P:(t + 1) * P],
                                     XIN[:, lo // P + t, m * P:(m + 1) * P], ID[:, :])
                x.then_inc(tr_done, 1)

        te.wait_ge(flt_in, 16 * 8)
        for n in range(2):
            if n:
                te.wait_ge(f_sin, 1)
            for s in range(2):
                lo, w = SEGS[s]
                x = te.matmul(PS[4 + s][0:FH, 0:w], (FW1, FW2)[n][:, :], (FEATS, FS)[n][:, lo:lo + w], start=True, stop=True)
            x.then_inc(f_pe, 1)
        te.wait_ge(f_sin, 2)
        for t in range(TB):
            if t >= 2:
                te.wait_ge(f_win, 2 * (t - 1))
            for v in range(2):
                te.matmul(PS[4 + 2 * (t % 2) + v][:, :], FS[:, t * P:(t + 1) * P], FW3[:, v * HY:(v + 1) * HY],
                          start=True, stop=True).then_inc(f_pe, 1)

        def spectra(n):
            k, b = FREQ[n]
            T, blocks, t0 = (FWDL, LB, 0) if k == 0 else (FWDC, CB_, LB)
            if n < 2:
                te.wait_ge(f_win, 2 * TB)
            else:
                te.wait_ge(f_spec, 2 * (n - 1))
            te.wait_ge(f_filt, 2 * TB)
            for v in range(2):
                for t in range(blocks):
                    x = te.matmul(PS[4 + 2 * (n % 2) + v][:, :], T[:, b, t, v, :], FILT[:, t0 + t, v, :],
                                  start=(t == 0), stop=(t == blocks - 1))
                x.then_inc(f_pe, 1)

        te.wait_ge(tab_in, 16 * 7)
        for n in range(NF):
            spectra(n)

        def ada_products(n, ks=range(KC)):
            if ks[0] == 0 and not (isinstance(n, int) and n == 0):
                te.wait_ge(ada_row, n)
            for k in ks:
                slot = k % ADA_RING
                te.wait_ge(ada_in[slot], 16 * (2 * n + k // ADA_RING + 1))
                for j in range(4):
                    x = te.matmul(PS[3][32 * j:32 * j + 32, 0:D // 4], SC[:, k, :],
                                  ADA[slot][:, j * D // 4:(j + 1) * D // 4], start=(k == 0), stop=(k == KC - 1))
                    if k == KC - 1 and j == 3:
                        x.then_inc(ada_sum, 1)
                    elif j == 3:
                        x.then_inc(ada_used, 1)

        def ada_columns(n):
            te.wait_ge(ada_row, n + 1)
            if not (isinstance(n, int) and n == 0):
                te.wait_ge(mod_ok, n)
            for q in range(2):
                te.transpose(PS[4][:, q * P:(q + 1) * P], ADAP[:, q * P:(q + 1) * P], ID[:, :])\
                    .then_inc((ada_used, ada_tr)[q], 1)

        te.wait_ge(cond_ok, 2)
        te.wait_ge(tr_taken, plan["ada_first"].tr)
        te.wait_ge(f_spec, 2 * NF)
        for g in range(ADA_FIRST):
            ada_products(g)
            ada_columns(g)

        def product(out, parts, k_of, x_hi, x_lo, wait=None):
            ks = len(parts)
            for k, (w_hi, w_lo) in enumerate(parts):
                if wait is not None:
                    wait(k)
                te.matmul(out, w_hi, x_hi(k), start=(k == 0), stop=False)
                te.matmul(out, w_hi, x_lo(k), start=False, stop=False)
                x = te.matmul(out, w_lo, x_hi(k), start=False, stop=(k == ks - 1))
            return x

        def ffn(name, S, ada):
            p = plan[name]

            def up(slot, i, first=False, down_before=False):
                b = 0 if slot == "A" else 3
                base = p.A if slot == "A" else p.B
                q = p.q + (0 if first else -2) if slot == "A" else p.q + 2
                if not (isinstance(i, int) and p.gs + i == 0):
                    te.wait_ge(mul[slot], p.gs + S * i)
                w = [t[slot][:, :].rearrange("p (s k n) -> p s k n", k=KC, s=2) for t in (WHI, WLO)]
                for s in range(S):
                    lo, n = SEGS[s]
                    for part in range(2):
                        out = PS[b + part][:, 0:LAT] if s == 0 else PS[b + 2][:, part * CTX:part * CTX + CTX]

                        def wait(k, s=s, part=part):
                            if s == 0 and k == 0:
                                te.wait_ge(lo_done, q + part + 1 + 6 * i)
                            if s == 1 and k == 0 and part == 0 and slot == "B" and down_before:
                                te.wait_ge(evac, p.evac + KC * S * i)
                            if first and slot == "A" and part == 0:
                                te.wait_ge(h_lo, p.h - KC * S + s * KC + k + 1)
                        x = product(out, [(w[0][:, part, k, :], w[1][:, part, k, :]) for k in range(KC)], None,
                                    lambda k: HHI[:, k, lo:lo + n], lambda k: HLO[:, k, lo:lo + n], wait)
                    x.then_inc(pe[slot], 1)

            def down(i, ada=False, last=False):
                g0 = p.g + i + 1
                te.wait_ge(glo["A"], g0)
                te.wait_ge(glo["B"], g0)
                te.wait_ge(lo_done, p.q + 8 + 6 * i - (2 if last else 0))
                w = [t["W"][:, :].rearrange("p (c m n) -> p c m n", c=2, m=KC) for t in (WHI, WLO)]
                for e, (m, s) in enumerate(down_groups(S)):
                    if ada and e == 5:
                        ada_products(ada_n[0], range(ADA_RING, KC))
                    if ada and e == 11:
                        ada_columns(ada_n[0])
                    lo, n = SEGS[s]
                    before = {0: e - 2 * S + 1, 1: e - 2}[s]
                    if (before > 0 or S == 1) and not (s == 1 and m % 2):
                        te.wait_ge(evac, p.evac + KC * S * i + before)
                    x = product(down_bank(m, s), [(w[0][:, c, m, :], w[1][:, c, m, :]) for c in range(2)], None,
                                lambda c: GHI["AB"[c]][:, lo:lo + n], lambda c: GLO["AB"[c]][:, lo:lo + n])
                    x.then_inc(pe["W"], 1)

            ada_n = [None]

            def body(i, first=False, ada=False):
                up("A", i, first)
                if ada:
                    te.wait_ge(mul["B"], p.gs + S * i)
                    ada_n[0] = p.ada + i - 1
                    ada_products(p.ada + i - 1, range(ADA_RING))
                if not first:
                    down(i - 1, ada)
                    if ada:
                        te.wait_ge(mod_ok, p.ada + i)
                up("B", i, down_before=not first)

            body(0, first=True)
            if ada:
                with te.Fori(1, 1 + ada) as i:
                    body(i, ada=True)
            if 1 + ada < FI - 1:
                with te.Fori(1 + ada, FI - 1) as i:
                    body(i)
            body(FI - 1)
            down(FI - 1, last=True)

        def layernorm(name, S, banks=(0, 3)):
            p = plan[name]
            for s in range(S):
                lo, n = SEGS[s]
                if s == 1:
                    te.wait_ge(evac, p.evac)
                for m in range(KC):
                    if s == 0:
                        te.wait_ge(evac, p.evac - S * KC + 4 * (m // 2) + m % 2 + 1 if S == 2 else p.evac - KC + m + 1)
                    x = te.matmul(PS[banks[s]][:, 0:n], ONES[:, :], X[:, m, lo:lo + n], start=(m == 0), stop=(m == KC - 1))
                x.then_inc(ln_pe, 1)
            for s in range(S):
                lo, n = SEGS[s]
                te.wait_ge(ln_mu, p.ln + s + 1)
                for m in range(KC):
                    te.wait_ge(ln_sq, KC * (p.ln + s) + m + 1)
                    x = te.matmul(PS[banks[s]][:, 0:n], ONES[:, :], SQ[:, m, lo:lo + n], start=(m == 0), stop=(m == KC - 1))
                x.then_inc(ln_pe, 1)

        def project(name, S, iters, order, ready, taken, per):
            p = plan[name]

            def body(i, first=False):
                for n, slot in enumerate("AB"):
                    b = 3 * n
                    w = [t[slot][:, :].rearrange("p (s k n) -> p s k n", k=KC, s=2) for t in (WHI, WLO)]
                    if not first:
                        te.wait_ge(taken, per * (2 * i + n - 1) + (p.taken if taken is mx_taken else p.evac))
                    for s in range(S):
                        lo, width = SEGS[s]
                        for half in range(2):
                            out = PS[b + half][:, 0:LAT] if s == 0 else PS[b + 2][:, CTX * half:CTX * half + CTX]
                            if s == 0:
                                te.wait_ge(lo_done, p.q + 2 * n + half + 1 + 4 * i)

                            def wait(k):
                                if first and n == 0 and half == 0:
                                    ready(order[k], s)
                            x = product(out, [(w[0][:, half, k, :], w[1][:, half, k, :]) for k in order], None,
                                        lambda k: HHI[:, order[k], lo:lo + width], lambda k: HLO[:, order[k], lo:lo + width], wait)
                            if s == 0 or half == 1:
                                x.then_inc(pe[slot], 1)

            body(0, True)
            if iters > 2:
                with te.Fori(1, iters) as i:
                    body(i)
            else:
                body(1)

        def h_ready(name, S):
            h = plan[name].h

            def ready(k, s):
                te.wait_ge(h_lo, h - KC * S + s * KC + k + 1)
            return ready

        def even_mixer():
            project("ev_in", 2, 5, list(range(KC)), h_ready("ev_in", 2), mx_taken, 4)
            te.wait_ge(mx_taken, 40)
            te.wait_ge(conv, CONV_END[11])
            for t in range(TB):
                s, b = (0, t) if t < LB else (1, t - LB)
                if t >= 4:
                    te.wait_ge(ut_ok, t - 3)
                for c in range(HC):
                    at = GSEGS[s][0] + b * P
                    x = te.transpose(PS[4 + t % 4][:, c * P:(c + 1) * P], U[:, c, at:at + P], ID[:, :])
                x.then_inc(ut_pe, 1)

            def gates(n):
                c, d = n // 2, n % 2
                te.wait_ge(bd_in[n % 2], 64 * (n // 2 + 1))
                if n:
                    te.wait_ge(r_sig, 4 * n)
                for s in range(2):
                    lo, w = GSEGS[s]
                    for v in range(2):
                        out = PS[v][:, 0:LAT] if s == 0 else PS[2][:, CTX * v:CTX * v + CTX]
                        x = te.matmul(out, BD[n % 2][:, v, :], XC[:, c, lo:lo + w], start=True, stop=True)
                    x.then_inc(gate_pe, 1)

            def forward(n):
                k, b = FREQ[n]
                blocks, t0 = (LB, 0) if k == 0 else (CB_, LB)
                te.wait_ge(slab_in[n % 2], 16 * (n // 2 + 1))
                te.wait_ge(ut_ok, TB)
                if n >= 2:
                    te.wait_ge(df_y, 4 * (n - 1))
                for v in range(2):
                    for t in range(blocks):
                        at = (2 * t + v) * P
                        x = te.matmul(PS[4 + 2 * (n % 2) + v][:, :], SLAB[n % 2][:, at:at + P], UT[:, t0 + t, :],
                                      start=(t == 0), stop=(t == blocks - 1))
                x.then_inc(df_pe, 1)

            for n in range(2 * HC):
                gates(n)
                if n < NF:
                    forward(n)
            te.wait_ge(df_y, 4 * NF)
            te.wait_ge(r_sig, 8 * HC)
            n = NF
            te.wait_ge(slab_in[n % 2], 16 * (n // 2 + 1))
            for c in range(HC):
                for b in range(CB_):
                    for v in range(2):
                        at = (2 * b + v) * CTX
                        x = te.matmul(PS[c // 2][:, CTX * (c % 2):CTX * (c % 2) + CTX], YC[v][:, b, c * P:(c + 1) * P],
                                      SLAB[n % 2][:, at:at + CTX], start=(b == 0 and v == 0), stop=(b == CB_ - 1 and v == 1))
                x.then_inc(inv_pe, 1)
            for b in range(LB):
                n = NF + 1 + b
                te.wait_ge(slab_in[n % 2], 16 * (n // 2 + 1))
                for c in range(HC):
                    for v in range(2):
                        x = te.matmul(PS[4 + c][:, :], YL[:, v, b, c * P:(c + 1) * P], SLAB[n % 2][:, v * LAT:(v + 1) * LAT],
                                      start=(b == 0 and v == 0), stop=(b == LB - 1 and v == 1))
                x.then_inc(inv_pe, 1)

            def ready(k, s):
                if k >= HC:
                    te.wait_ge(y_rg, 2 * (k - HC + 1))
                else:
                    te.wait_ge(y_hy, HC * s + k + 1)
            te.wait_ge(hy_t, 2 * NF + 2 * HC)
            project("ev_out", 2, 2, [4, 5, 6, 7, 0, 1, 2, 3], ready, evac, 4)

        ffn("ffn0", 2, N_ADA - ADA_FIRST)
        layernorm("ln0", 2)
        even_mixer()
        layernorm("ln1", 2, (6, 7))
        ffn("ffn1", 2, N_ADA)
        layernorm("ln2", 2)
        ffn("ffn2", 2, 0)
        layernorm("ln3", 2)

        def odd_mixer():
            p = plan["mla_in"]
            ready = h_ready("mla_in", 2)
            kk = list(range(KC))
            free = [0, 0, 4, 5, 7]
            for u in range(5):
                slot, b = "AB"[u % 2], 3 * (u % 2)
                halves = 1 if u == 1 else 2
                M = 2 * ROPE if u == 1 else P
                if u == 1:
                    w = [t["B"][:, 0:KC * M].rearrange("p (s k n) -> p s k n", k=KC, s=1) for t in (WHI, WLO)]
                else:
                    w = [t[slot][:, :].rearrange("p (s k n) -> p s k n", k=KC, s=2) for t in (WHI, WLO)]
                if free[u]:
                    te.wait_ge(m_taken, free[u])
                if u == 3:
                    te.wait_ge(krp, 2)
                for s in range(2 if u < 2 else 1):
                    lo, n = SEGS[s]
                    for half in range(halves):
                        out = PS[b + half][0:M, 0:LAT] if s == 0 else PS[b + 2][0:M, CTX * half:CTX * half + CTX]
                        if s == 0:
                            te.wait_ge(lo_done, p.q + MLA_HALF[u] + half + 1)
                        x = product(out, [(w[0][:, half, k, :], w[1][:, half, k, :]) for k in kk], None,
                                    lambda k: HHI[:, k, lo:lo + n], lambda k: HLO[:, k, lo:lo + n],
                                    (lambda k: ready(k, s)) if u == 0 and half == 0 else None)
                        if s == 0 or half == halves - 1:
                            x.then_inc(pe[slot], 1)

            done = 0
            for e, (T, chunks, lo, n, rs, width) in enumerate(RMS):
                if e == 2:
                    te.wait_ge(mr_std, 1)
                for c in range(chunks):
                    done += 1
                    te.wait_ge(mr_sq, done)
                    x = te.matmul(PS[6 + e % 2][:, 0:n], ONES[:, :], SQQ[:, c, 0:n], start=(c == 0), stop=(c == chunks - 1))
                x.then_inc(mr_pe, 1)

            te.wait_ge(v_lo, 1)
            te.wait_ge(mr_lo, 2 * KVC)
            for t in range(2 * TB):
                tok, cols = slice(P * (t // 2), P * (t // 2) + P), slice(512 * (t % 2), 512 * (t % 2) + 512)
                if t >= 4:
                    te.wait_ge(v_tl, t - 3)
                product(PS[t % 4][:, :], [(KVH[:, k, tok], KVL_[:, k, tok]) for k in range(KVC)], None,
                        lambda k: WVH[:, k, cols], lambda k: WVL[:, k, cols]).then_inc(v_pe, 1)

            def proj_piece(z, h, piece):
                if piece == 0:
                    te.wait_ge(wq_ok, h + 1)
                    if not (isinstance(h, int) and h == 0):
                        te.wait_ge(k_lo, 2 * h)
                    product(PS[7][:, :], [(WQH[z][:, k, :], WQL[z][:, k, :]) for k in range(QC_)], None,
                            lambda k: QNH[:, k, :], lambda k: QNL[:, k, :]).then_inc(q_pe, 1)
                else:
                    lo, n = SEGS[piece - 1]
                    if piece == 1:
                        te.wait_ge(q_rot, 2 * h + 2)
                        te.wait_ge(q_cp, h + 1)
                    else:
                        te.wait_ge(k_lo, 2 * h + 1)
                    product(PS[7][0:NOPE, 0:n], [(WKH[z][:, k, :], WKL[z][:, k, :]) for k in range(KVC)], None,
                            lambda k: KVH[:, k, lo:lo + n], lambda k: KVL_[:, k, lo:lo + n]).then_inc(k_pe, 1)

            def scores(i, s):
                g, z, t = 8 * i + s, s // QT_, s % QT_
                if t == 0:
                    te.wait_ge(q_lo, 2 * i + z + 1)
                    te.wait_ge(k_lo, 2 * (2 * i + z) + 2)
                if not (isinstance(g, int) and g < 2):
                    te.wait_ge(s_exp, g - 1)
                tok = slice(P * t, P * t + P)
                for lo, n in SEGS:
                    x = product(SC_(s)[:, lo:lo + n], [(QH[z][0:QD, tok], QLO[z][0:QD, tok])], None,
                                lambda k: KH[z][0:QD, lo:lo + n], lambda k: KLO[z][0:QD, lo:lo + n])
                x.then_inc(s_pe, 1)

            def turn(i, s):
                g = 8 * i + s
                te.wait_ge(s_norm, g + 1)
                if not (isinstance(g, int) and g == 0):
                    te.wait_ge(pt_lo, g)
                for t in range(TB):
                    x = te.matmul(TR_[:, t, :], PR[s % 2][:, t * P:(t + 1) * P], DIAG[s % 2][:, :], start=True, stop=True)
                x.then_inc(t_pe, 1)

            def outputs(i, e):
                z, half = (e // 2) % 2, e % 2
                te.wait_ge(pt_lo, 8 * i + 2 * e + 2)
                te.wait_ge(vs_ok, 2 * (2 * i + e // 2) + 2)
                if not (isinstance(i, int) and 4 * i + e == 0):
                    te.wait_ge(o_cp, 4 * i + e)
                product(PS[6][0:VD, 0:CTX], [(VSH[z][:, t, :], VSL[z][:, t, :]) for t in range(TB)], None,
                        lambda t: PTH[half][:, t, :], lambda t: PTL[half][:, t, :]).then_inc(av_pe, 1)

            def body(i, first=False, last=False):
                for s in range(2 * QT_):
                    z = s // QT_
                    if s % 4 > 0 and not (last and z == 1):
                        proj_piece(1 - z, 2 * i + z + 1, s % 4 - 1)
                    scores(i, s)
                    if s % 2 == 0 and not (first and z == 0):
                        outputs(i, s // 2 - 2)
                    if not (first and s == 0):
                        turn(i, s - 1)

            te.wait_ge(kr, 3)
            te.wait_ge(mr_lo, 2 * KVC + QC_)
            for piece in range(3):
                proj_piece(0, 0, piece)
            body(0, first=True)
            with te.Fori(1, MH // 2 - 1) as i:
                body(i)
            body(MH // 2 - 1, last=True)
            turn(MH // 2 - 1, 7)
            for e in (2, 3):
                outputs(MH // 2 - 1, e)

            project("mla_out", 1, 2, kk, lambda k, s: te.wait_ge(och_lo, k + 1), evac, 2)

        odd_mixer()
        layernorm("ln4", 1, (6,))
        ffn("ffn3", 1, 0)
        layernorm("final", 1, (0,))
        te.wait_ge(fin_x, KC)
        for t in range(LAT // P):
            for half in range(2):
                e = 2 * t + half
                if e >= 4:
                    te.wait_ge(fin_cp, e - 3)
                for m in range(4):
                    x = te.transpose(PS[2 + e % 4][:, m * P:(m + 1) * P], X[:, 4 * half + m, t * P:(t + 1) * P], ID[:, :])
                x.then_inc(fin_tr, 1)

    stack.close()


_INS = ("x", "c", "ctx", "c_ctx", "ada_w", "ada_b", "ln_g", "ln_b", "ffn_w_in", "ffn_w_out", "ev_w_in", "ev_w_out",
        "hy_conv_w", "hy_conv_b", "hy_filt_w1", "hy_filt_b1", "hy_filt_w2", "hy_filt_b2", "hy_filt_w3", "hy_sin_freq",
        "hy_bias", "rg_conv_w", "rg_conv_b", "rg_a_w", "rg_a_b", "rg_x_w", "rg_x_b", "rg_lambda", "mla_w_in",
        "mla_q_norm", "mla_kv_norm", "mla_w_q_up", "mla_w_kv_up", "mla_w_out")


def kernel(**inputs):
    import numpy as _np
    import concourse.bacc as _bacc
    from concourse import mybir as _mybir
    from concourse.bass_utils import run_bass_kernel_spmd as _run

    nc = _bacc.Bacc("TRN2", target_bir_lowering=False, num_devices=1)
    arrays, args = {}, {}
    tables = constants()
    for name in _INS + tuple(tables):
        a = _np.ascontiguousarray(tables[name] if name in tables else inputs[name])
        arrays[f"in_{name}_dram"] = a
        args[name] = nc.dram_tensor(f"in_{name}_dram", a.shape, _mybir.dt.from_np(a.dtype), kind="ExternalInput").ap()
    out = nc.dram_tensor("out_dram", (1, LAT, D), _mybir.dt.float32, kind="ExternalOutput").ap()
    build(nc, args, out)
    r = _run(nc, [arrays], core_ids=[0])
    return r.results[0]["out_dram"]
```
